# Optimizing a Trainium2 kernel written in Bass

```python
import math
import jax, jax.numpy as jnp
from jax import lax
import numpy as np

D_MODEL = 1024
BATCH = 1
SEQ = 256
DEPTH = 1

HEAD_DIM = 64
N_HEADS_MOBA = D_MODEL // HEAD_DIM // 2
N_HEADS_SWA = D_MODEL // HEAD_DIM // 2
N_KV_SWA = 2
N_HEADS = N_HEADS_MOBA + N_HEADS_SWA
D_MOBA = N_HEADS_MOBA * HEAD_DIM
D_SWA_Q = N_HEADS_SWA * HEAD_DIM
D_SWA_KV = N_KV_SWA * HEAD_DIM
D_MIX = D_MOBA + D_SWA_Q
D_IN = 3 * D_MOBA + D_SWA_Q + 2 * D_SWA_KV
MOBA_BLOCK = 256
MOBA_TOPK = 3
MOBA_QCHUNK = 32
SWA_WINDOW = 128
SWA_BLOCK = 128
REL_BUCKETS = 32
REL_MAX_DIST = 1024
N_EXPERTS = 32
TOP_K = 4
D_FF = 1024
SWIGLU_LIMIT = 7.0
SWIGLU_ALPHA = 1.702
EPS = 1e-5
NEG = -1e30

kernel_name = "hymba_moba_swa_sink_moe_adaln"

def rmsnorm(x, g):
    xf = x.astype(jnp.float32)
    y = xf * lax.rsqrt(jnp.mean(xf * xf, axis=-1, keepdims=True) + EPS)
    return (y * g.astype(jnp.float32)).astype(x.dtype)

def rel_bucket(dist):
    max_exact = REL_BUCKETS // 2
    n = jnp.maximum(dist, 0)
    nf = jnp.maximum(n, 1).astype(jnp.float32)
    large = max_exact + (jnp.log(nf / max_exact) / math.log(REL_MAX_DIST / max_exact)
                         * (REL_BUCKETS - max_exact)).astype(jnp.int32)
    large = jnp.minimum(large, REL_BUCKETS - 1)
    return jnp.where(n < max_exact, n, large)

def moba_attention(q, k, v, rel_table):
    B, S, H, Dh = q.shape
    L = MOBA_BLOCK
    Sp = -(-S // L) * L
    pad = Sp - S
    if pad:
        q, k, v = [jnp.pad(a, ((0, 0), (0, pad), (0, 0), (0, 0))) for a in (q, k, v)]
    nb = Sp // L
    kbh = k.reshape(B, nb, L, H, Dh).transpose(0, 3, 1, 2, 4)
    vbh = v.reshape(B, nb, L, H, Dh).transpose(0, 3, 1, 2, 4)
    kmean = jnp.mean(kbh.astype(jnp.float32), axis=3)
    gate = jnp.einsum('bshd,bhnd->bhsn', q.astype(jnp.float32), kmean)
    qblk = jnp.arange(Sp) // L
    past = jnp.arange(nb)[None, :] < qblk[:, None]
    gate = jnp.where(past, gate, NEG)
    kk = min(MOBA_TOPK, nb)
    _, sel = lax.top_k(gate, kk)
    QC = MOBA_QCHUNK
    nc = Sp // QC
    q_all = q.reshape(B, nc, QC, H, Dh).transpose(1, 0, 2, 3, 4)
    sel_all = sel.reshape(B, H, nc, QC, kk).transpose(2, 0, 1, 3, 4)
    table_h = rel_table.T
    b_ix = jnp.arange(B)[:, None, None, None]
    h_ix = jnp.arange(H)[None, :, None, None]
    offs = jnp.arange(L)
    scale = Dh ** -0.5

    def chunk(args):
        qc, selc, ci = args
        start = ci * QC
        qpos = start + jnp.arange(QC)
        own = start // L
        kg = kbh[b_ix, h_ix, selc]
        vg = vbh[b_ix, h_ix, selc]
        s_past = jnp.einsum('bqhd,bhqjld->bhqjl', qc, kg,
                            preferred_element_type=jnp.float32) * scale
        kpos = selc[..., None] * L + offs
        s_past = s_past + table_h[h_ix[..., None], rel_bucket(qpos[:, None, None] - kpos)].astype(jnp.float32)
        valid = jnp.arange(kk) < own
        s_past = jnp.where(valid[:, None], s_past, NEG)
        kown = lax.dynamic_index_in_dim(kbh, own, axis=2, keepdims=False)
        vown = lax.dynamic_index_in_dim(vbh, own, axis=2, keepdims=False)
        s_own = jnp.einsum('bqhd,bhld->bhql', qc, kown,
                           preferred_element_type=jnp.float32) * scale
        dist_own = qpos[:, None] - (own * L + offs)[None, :]
        s_own = jnp.where(dist_own >= 0,
                          s_own + table_h[:, rel_bucket(dist_own)][None].astype(jnp.float32), NEG)
        logits = jnp.concatenate([s_past.reshape(B, H, QC, kk * L), s_own], axis=-1)
        p = jax.nn.softmax(logits, axis=-1)
        p_past = p[..., :kk * L].reshape(B, H, QC, kk, L).astype(v.dtype)
        p_own = p[..., kk * L:].astype(v.dtype)
        return (jnp.einsum('bhqjl,bhqjld->bqhd', p_past, vg)
                + jnp.einsum('bhql,bhld->bqhd', p_own, vown))

    out = lax.map(chunk, (q_all, sel_all, jnp.arange(nc)))
    return out.transpose(1, 0, 2, 3, 4).reshape(B, Sp, H, Dh)[:, :S]

def swa_attention(q, k, v, sinks, rel_table):
    B, S, Hq, Dh = q.shape
    Hkv = k.shape[2]
    G = Hq // Hkv
    W = SWA_BLOCK
    nq = S // W
    qb = q.reshape(B, nq, W, Hkv, G, Dh)

    def band(a):
        prev = jnp.pad(a, ((0, 0), (W, 0), (0, 0), (0, 0)))[:, :S]
        return jnp.concatenate([prev.reshape(B, nq, W, Hkv, Dh),
                                a.reshape(B, nq, W, Hkv, Dh)], axis=2)

    kw, vw = band(k), band(v)
    s = jnp.einsum('bnqhgd,bnkhd->bnhgqk', qb, kw,
                   preferred_element_type=jnp.float32) * Dh ** -0.5
    qi = jnp.arange(W)
    ki = jnp.arange(2 * W)
    dist = qi[:, None] + W - ki[None, :]
    kpos = jnp.arange(nq)[:, None] * W - W + ki[None, :]
    allowed = (dist >= 0) & (dist < SWA_WINDOW) & (kpos[:, None, :] >= 0)
    bias = rel_table[rel_bucket(dist)].astype(jnp.float32).transpose(2, 0, 1).reshape(Hkv, G, W, 2 * W)
    s = jnp.where(allowed[None, :, None, None], s + bias, NEG)
    sink = jnp.broadcast_to(sinks.astype(jnp.float32).reshape(Hkv, G, 1, 1), s.shape[:-1] + (1,))
    p = jax.nn.softmax(jnp.concatenate([s, sink], axis=-1), axis=-1)[..., :-1].astype(v.dtype)
    o = jnp.einsum('bnhgqk,bnkhd->bnqhgd', p, vw)
    return o.reshape(B, S, Hq, Dh)

def moe_ffn(h, w_router, b_router, w_gate_up, b_gate_up, w_down, b_down):
    B, S, D = h.shape
    t = h.reshape(B * S, D)
    logits = (t @ w_router + b_router).astype(jnp.float32)
    top_val, top_idx = lax.top_k(logits, TOP_K)
    top_w = jax.nn.softmax(top_val, axis=-1)
    combine = jnp.sum(jax.nn.one_hot(top_idx, N_EXPERTS, dtype=jnp.float32) * top_w[..., None], axis=1)
    out = jnp.zeros((B * S, D), jnp.float32)
    for e in range(N_EXPERTS):
        gu = t @ w_gate_up[e] + b_gate_up[e]
        g = jnp.minimum(gu[:, :D_FF], SWIGLU_LIMIT)
        u = jnp.clip(gu[:, D_FF:], -SWIGLU_LIMIT, SWIGLU_LIMIT)
        y = ((u + 1) * (g * jax.nn.sigmoid(SWIGLU_ALPHA * g))) @ w_down[e] + b_down[e]
        out = out + combine[:, e:e + 1] * y
    return out.astype(h.dtype).reshape(B, S, D)

def setup_inputs(seed: int = 0) -> dict:
    key = jax.random.key(seed)
    ks = jax.random.split(key, 20)
    f32 = jnp.float32

    def nrm(k, shape, s):
        return jax.random.normal(k, shape, f32) * s

    return {
        "x": nrm(ks[0], (BATCH, SEQ, D_MODEL), 1.0),
        "c": nrm(ks[1], (BATCH, D_MODEL), 1.0),
        "g_attn": 1.0 + nrm(ks[2], (DEPTH, D_MODEL), 0.02),
        "w_ada": nrm(ks[3], (DEPTH, D_MODEL, 6 * D_MODEL), 0.5 * D_MODEL ** -0.5),
        "b_ada": nrm(ks[4], (DEPTH, 6 * D_MODEL), 0.02),
        "w_in": nrm(ks[5], (DEPTH, D_MODEL, D_IN), D_MODEL ** -0.5),
        "b_in": nrm(ks[6], (DEPTH, D_IN), 0.02),
        "w_out": nrm(ks[7], (DEPTH, D_MIX, D_MODEL), D_MIX ** -0.5),
        "b_out": nrm(ks[8], (DEPTH, D_MODEL), 0.02),
        "rel_table": nrm(ks[9], (REL_BUCKETS, N_HEADS), 0.5),
        "sinks": nrm(ks[10], (DEPTH, N_HEADS_SWA), 1.0),
        "g_ffn": 1.0 + nrm(ks[11], (DEPTH, D_MODEL), 0.02),
        "w_router": nrm(ks[12], (DEPTH, D_MODEL, N_EXPERTS), D_MODEL ** -0.5),
        "b_router": nrm(ks[13], (DEPTH, N_EXPERTS), 0.01),
        "w_gate_up": nrm(ks[14], (DEPTH, N_EXPERTS, D_MODEL, 2 * D_FF), D_MODEL ** -0.5),
        "b_gate_up": nrm(ks[15], (DEPTH, N_EXPERTS, 2 * D_FF), 0.02),
        "w_down": nrm(ks[16], (DEPTH, N_EXPERTS, D_FF, D_MODEL), D_FF ** -0.5),
        "b_down": nrm(ks[17], (DEPTH, N_EXPERTS, D_MODEL), 0.02),
        "g_final": 1.0 + nrm(ks[18], (D_MODEL,), 0.02),
    }

def reference(x, c, g_attn, w_ada, b_ada, w_in, b_in, w_out, b_out, rel_table, sinks,
              g_ffn, w_router, b_router, w_gate_up, b_gate_up, w_down, b_down, g_final):
    B, S, D = x.shape
    sc = jax.nn.silu(c)
    for l in range(DEPTH):
        mod = sc @ w_ada[l] + b_ada[l]
        shift_a, scale_a, gate_a, shift_f, scale_f, gate_f = [m[:, None, :] for m in jnp.split(mod, 6, axis=-1)]

        h = rmsnorm(x, g_attn[l]) * (1 + scale_a) + shift_a
        proj = h @ w_in[l] + b_in[l]
        i0 = D_MOBA
        i1 = 2 * D_MOBA
        i2 = 3 * D_MOBA
        i3 = i2 + D_SWA_Q
        i4 = i3 + D_SWA_KV
        q_m = proj[..., :i0].reshape(B, S, N_HEADS_MOBA, HEAD_DIM)
        k_m = proj[..., i0:i1].reshape(B, S, N_HEADS_MOBA, HEAD_DIM)
        v_m = proj[..., i1:i2].reshape(B, S, N_HEADS_MOBA, HEAD_DIM)
        q_s = proj[..., i2:i3].reshape(B, S, N_HEADS_SWA, HEAD_DIM)
        k_s = proj[..., i3:i4].reshape(B, S, N_KV_SWA, HEAD_DIM)
        v_s = proj[..., i4:].reshape(B, S, N_KV_SWA, HEAD_DIM)
        o_m = moba_attention(q_m, k_m, v_m, rel_table[:, :N_HEADS_MOBA])
        o_s = swa_attention(q_s, k_s, v_s, sinks[l], rel_table[:, N_HEADS_MOBA:])
        o = jnp.concatenate([o_m.reshape(B, S, D_MOBA), o_s.reshape(B, S, D_SWA_Q)], axis=-1)
        x = x + gate_a * (o @ w_out[l] + b_out[l])

        h = rmsnorm(x, g_ffn[l]) * (1 + scale_f) + shift_f
        x = x + gate_f * moe_ffn(h, w_router[l], b_router[l], w_gate_up[l], b_gate_up[l],
                                 w_down[l], b_down[l])
    return rmsnorm(x, g_final)


_drawn_inputs = setup_inputs


def setup_inputs(seed=0):
    import zlib

    import numpy as np

    out = dict(_drawn_inputs(seed))
    spreads = {}
    factors = {'g_attn': 7.695,
     'b_in': 6.587,
     'b_out': 5.025,
     'sinks': 23.02,
     'g_ffn': 3.731,
     'b_router': 5.731,
     'b_gate_up': 8.0,
     'b_down': 42.863,
     'g_final': 8.498}
    for name, (base, spread) in spreads.items():
        noise = np.random.default_rng([zlib.crc32(name.encode()), seed]).standard_normal(out[name].shape)
        drawn = base * np.exp(spread * noise) if base else spread * noise
        out[name] = __import__('jax').numpy.asarray(drawn.astype(out[name].dtype))
    for name, factor in factors.items():
        out[name] = (out[name] * factor).astype(out[name].dtype)
    return out
```

```python
from contextlib import ExitStack
import math

import concourse.bass as bass
from concourse import mybir
import numpy as np

P = 128
D = 1024
S = 256
TT = S // P
KT = D // P
DH = 64
NH = 16
NHM = 8
QK_COLS = 512
D_IN = 2304
NE = 32
TOPK = 4
FF = 1024
LIMIT = 7.0
ALPHA = 1.702
EPS = 1e-5
NEG = -1e30
BIG = 3.0e38
BUCKETS = 32
MAX_DIST = 1024
WINDOW = 128

SLOTS = 64
ROUNDS = S // SLOTS
RING = 8
CW = 512
EPB = 4
CPE = 6
ITERS = NE // EPB
HB = 4

F32 = mybir.dt.float32
I32 = mybir.dt.int32
ALU = mybir.AluOpType
ACT = mybir.ActivationFunctionType
AX = mybir.AxisListType

SHIFT_A, SCALE_A, GATE_A, SHIFT_F, SCALE_F, GATE_F = range(6)
ADA_PE = [("ada", SCALE_A * D), ("ada", SCALE_A * D + CW), ("ada", SHIFT_A * D), ("ada", SHIFT_A * D + CW)]
ADA_DVE = [("ada", part * D + half * CW) for part in (GATE_A, SHIFT_F, SCALE_F, GATE_F) for half in (0, 1)]
Q_M, K_M, V_M, Q_S, KV_S = [("in", CW * i) for i in range(5)]
HEAD_CHUNKS = ADA_PE + [Q_M, K_M, ADA_DVE[0], V_M, ADA_DVE[1], ADA_DVE[2], Q_S, ADA_DVE[3], ADA_DVE[4], KV_S,
                        ADA_DVE[5], ADA_DVE[6], ADA_DVE[7], ("out", 0), ("out", CW)]
PRE = len(HEAD_CHUNKS)


def bucket_table():
    hot = np.zeros((BUCKETS + 2, 384), np.float32)
    exact = BUCKETS // 2
    for m in range(384):
        d = 255 - m
        if d >= 0:
            if d < exact:
                b = d
            else:
                nf = np.float32(d) / np.float32(exact)
                b = exact + int(np.float32(np.log(nf)) / np.float32(math.log(MAX_DIST / exact)) * np.float32(BUCKETS - exact))
                b = min(b, BUCKETS - 1)
            hot[b, m] = 1.0
        hot[BUCKETS, m] = d < 0
        hot[BUCKETS + 1, m] = d < 0 or d >= WINDOW
    return hot


def mask_rows():
    rows = np.zeros((2, NH), np.float32)
    rows[0, :NHM] = NEG
    rows[1, NHM:] = NEG
    return rows


def build(nc, x, c_col, g_attn_col, w_ada, b_ada_col, b_ada_row, w_in, b_in_col, b_in_row, w_out, b_out, rel_table,
          sinks, g_ffn_col, w_router, b_router, w_gate_up, b_gate_up_col, w_down, b_down, g_final, bucket_hot, masks,
          toeplitz, out):
    with ExitStack() as ctx:
        def sb(name, shape, dt=F32):
            return ctx.enter_context(nc.sbuf_tensor(name, shape, dt))

        def sem(name):
            return ctx.enter_context(nc.semaphore(name))

        bank = [ctx.enter_context(nc.psum_tensor(f"bank{i}", [P, 512], F32)) for i in range(8)]

        ring = sb("ring", [P, RING, KT, CW])
        x_rows = sb("x_rows", [P, TT, D])
        xn_rows = sb("xn_rows", [P, TT, D])
        hT = sb("hT", [P, KT, S])
        gates = sb("gates", [P, 2, D])
        ident = sb("ident", [P, P])
        ones = sb("ones", [P, P])
        earlier = sb("earlier", [P, P])
        slot_no = sb("slot_no", [P, SLOTS])
        col = sb("col", [P, 160])
        c_sb, sc_sb = col[:, 0:8], col[:, 8:16]
        ga_sb, gf_sb = col[:, 16:24], col[:, 24:32]
        ba_sb = col[:, 32:80]
        bi_sb = col[:, 80:98]
        nbq_sb = col[:, 98:106]
        mul_a, add_a = col[:, 106:114], col[:, 114:122]
        mul_f, add_f = col[:, 122:130], col[:, 130:138]
        stat = sb("stat", [P, 16])
        sink_sb = sb("sink_sb", [P, NHM])
        nsink_sb = sb("nsink_sb", [P, NHM])
        table_sb = sb("table_sb", [BUCKETS + 2, NH])
        wr_sb = sb("wr_sb", [P, KT, NE])
        br_sb = sb("br_sb", [P, NE])
        lowest = sb("lowest", [P, NH, TT])
        rowsum = sb("rowsum", [P, NH, TT])
        sinkexp = sb("sinkexp", [P, NHM, TT])
        peak = sb("peak", [1, 2], I32)
        prob = sb("prob", [P, 2, 384])
        probT = sb("probT", [P, 2, 384])
        ada_acc = prob[:, :, :].rearrange("p a n -> p (a n)")[:, 0:512], probT[:, :, :].rearrange("p a n -> p (a n)")[:, 0:512]
        hot_sb = probT[0:BUCKETS + 2, 0, :]
        line_sb = prob[0:NH, 0, :]
        late = sb("late", [P, 8704])
        bias = late[:, 0:4096].rearrange("p (h n) -> p h n", h=NH)
        qT = late[:, 4096:6144].rearrange("p (b n) -> p b n", b=8)
        kT = late[:, 6144:7424].rearrange("p (b n) -> p b n", b=5)
        v_rows = late[:, 7424:8704].rearrange("p (t n) -> p t n", t=TT)

        used = [0]

        def piece(n):
            used[0] += n
            return late[:, used[0] - n:used[0]]

        xT_e = piece(2 * KT * SLOTS).rearrange("p (b k n) -> p b k n", b=2, k=KT)
        gu = piece(2 * 8 * SLOTS).rearrange("p (c g m n) -> p c g m n", c=2, g=2, m=HB)
        sig = piece(2 * HB * SLOTS).rearrange("p (c n) -> p c n", c=2)
        act = piece(KT * SLOTS).rearrange("p (k n) -> p k n", k=KT)
        yT = piece(KT * 2 * SLOTS).rearrange("p (k n) -> p k n", k=KT)
        y_rows = piece(D)
        gT = piece(S)
        bgu = piece(NE * 16).rearrange("p (e m) -> p e m", m=16)
        slot_of = piece(TT * (ROUNDS * NE + 2)).rearrange("p (t n) -> p t n", t=TT)
        weight_of = piece(TT * (ROUNDS * NE + 2)).rearrange("p (t n) -> p t n", t=TT)
        pick = piece(2 * TT * SLOTS).rearrange("p (b t n) -> p b t n", b=2, t=TT)
        put = piece(2 * TT * 2 * SLOTS).rearrange("p (b t n) -> p b t n", b=2, t=TT)
        bdown_sb = piece(D)[0:NE, :]
        route = piece(TT * 160).rearrange("p (t n) -> p t n", t=TT)
        assert used[0] <= 8704
        logit, left = route[:, :, 0:40], route[:, :, 40:76]
        top8, chosen, combine = route[:, :, 76:84], route[:, :, 84:116], route[:, :, 116:148]
        top_stat = route[:, :, 148:152]
        combT = gu[0:NE, 0, :, :, :].rearrange("p g m n -> p (g m n)")[:, 0:S]
        gfin = hT[:, 0:4, :].rearrange("p k n -> p (k n)")

        chunk_in = [sem(f"chunk_in{i}") for i in range(RING)]
        chunk_used = sem("chunk_used")
        x_in, vec_in, same_in, hot_in = sem("x_in"), sem("vec_in"), sem("same_in"), sem("hot_in")
        line_out, bias_in, b_out_in = sem("line_out"), sem("bias_in"), sem("b_out_in")
        late_in, gfin_in, result_out = sem("late_in"), sem("gfin_in"), sem("result_out")
        consts, line_ready, line_copied = sem("consts"), sem("line_ready"), sem("line_copied")
        dve = sem("dve")
        squares, means, roots = sem("squares"), sem("means"), sem("roots")
        sc_sig, sc_ready = sem("sc_sig"), sem("sc_ready")
        xn_ready, x_turned, hT_dve, hT_act = sem("xn_ready"), sem("x_turned"), sem("hT_dve"), sem("hT_act")
        mod_ready, ada_rows, ada_taken = sem("mod_ready"), sem("ada_rows"), sem("ada_taken")
        proj, proj_act, proj_dve = sem("proj"), sem("proj_act"), sem("proj_dve")
        scores, lows, exps, probs_ready = sem("scores"), sem("lows"), sem("exps"), sem("probs_ready")
        p_turned, pT_ready, o_ready, o_taken = sem("p_turned"), sem("pT_ready"), sem("o_ready"), sem("o_taken")
        mixed, x1_ready, xn1_ready, x1_turned = sem("mixed"), sem("x1_ready"), sem("xn1_ready"), sem("x1_turned")
        h2_dve, h2_act, logits_ready, top_ready = sem("h2_dve"), sem("h2_act"), sem("logits_ready"), sem("top_ready")
        top_exp, chosen_ready, places = sem("top_exp"), sem("chosen_ready"), sem("places")
        comb_ready, comb_turned, combT_ready = sem("comb_ready"), sem("comb_turned"), sem("combT_ready")
        routed = sem("routed")
        picks, gathered, xT_ready = sem("picks"), sem("gathered"), sem("xT_ready")
        gu_taken, gate_cut = sem("gu_taken"), sem("gate_cut")
        sig_ready, act_ready = sem("sig_ready"), sem("act_ready")
        dve_e = sem("dve_e")
        yT_ready, y_turned, y_ready = sem("yT_ready"), sem("y_turned"), sem("y_ready")
        g_turned, gT_ready, scattered = sem("g_turned"), sem("gT_ready"), sem("scattered")
        moe_done, x2_ready, fin_ready = sem("moe_done"), sem("x2_ready"), sem("fin_ready")

        block = ctx.enter_context(nc.Block())
        DVE_E = 5

        def wait_chunk(eng, n, it=None):
            landed = 16 * (n // RING + 1)
            eng.wait_ge(chunk_in[n % RING], landed if it is None else it * (16 * EPB * CPE // RING) + landed)

        def chunk_no(kind):
            return HEAD_CHUNKS.index(kind)

        JOB_CHUNK = [chunk_no(kind) for kind in (Q_M, K_M, V_M, Q_S, KV_S)]

        def job_signal(job):
            return (chunk_used if job % 2 else proj), 1

        def wait_job(eng, job):
            if job % 2:
                eng.wait_ge(chunk_used, JOB_CHUNK[job // 2] + 1)
            else:
                eng.wait_ge(proj, job // 2 + 1)

        def wait_experts(eng, it, e, chunks):
            eng.wait_ge(chunk_used, it * (EPB * CPE) + (PRE + CPE * e + chunks))

        def all_rounds(eng, body):
            with eng.Fori(0, ITERS) as p:
                body(p, p)
            eng.wait_ge(routed, 1)
            busiest = eng.value_load(peak[0:1, 0:1], min_val=1, max_val=S)
            with eng.If(busiest > SLOTS):
                with eng.Fori(1, (busiest + (SLOTS - 1)) // SLOTS) as r:
                    with eng.Fori(0, ITERS) as p:
                        body(r * ITERS + p, p)
            return (busiest + (SLOTS - 1)) // SLOTS * ITERS

        def head_of(h):
            return h if h < NHM else NHM + (h - NHM) // 2 + 4 * (h % 2)

        @block.sync
        def _(sp):
            source = {"ada": w_ada, "in": w_in, "out": w_out}
            for n, (kind, first) in enumerate(HEAD_CHUNKS):
                if n >= RING:
                    sp.wait_ge(chunk_used, n - RING + 1)
                w = min(CW, source[kind].shape[1] - first)
                sp.dma_start(ring[:, n % RING, :, 0:w],
                             source[kind][:, first:first + w].rearrange("(k p) n -> p k n", p=P)
                             ).then_inc(chunk_in[n % RING], 16)

            def load_experts(it, p):
                for e in range(EPB):
                    for j in range(CPE):
                        n = PRE + CPE * e + j
                        sp.wait_ge(chunk_used, it * (EPB * CPE) + (n - RING + 1))
                        if j < 4:
                            src = w_gate_up[bass.ds(p * EPB + e, 1), :, (j % 2) * FF + (j // 2) * CW:
                                            (j % 2) * FF + (j // 2 + 1) * CW]
                        else:
                            src = w_down[bass.ds(p * EPB + e, 1), :, (j - 4) * CW:(j - 3) * CW]
                        sp.dma_start(ring[:, n % RING], src.rearrange("a (k p) n -> p (a k) n", p=P)
                                     ).then_inc(chunk_in[n % RING], 16)

            all_rounds(sp, load_experts)
            for t in range(TT):
                sp.wait_ge(fin_ready, t + 1)
                sp.dma_start(out[t * P:(t + 1) * P, :], xn_rows[:, t, :]).then_inc(result_out, 16)
            sp.wait_ge(result_out, 16 * TT)

        @block.gpsimd
        def _(pool):
            pool.memset(ones[:, :], 1.0).then_inc(consts, 1)
            pool.wait_ge(consts, 1)
            pool.affine_select(out=ident[:, :], in_=ones[:, :], compare_op=ALU.is_equal, fill=0.0,
                               base=0, pattern=[[-1, P]], channel_multiplier=1).then_inc(consts, 1)
            pool.affine_select(out=earlier[:, :], in_=ones[:, :], compare_op=ALU.is_gt, fill=0.0,
                               base=0, pattern=[[1, P]], channel_multiplier=-1).then_inc(consts, 1)
            pool.iota(slot_no[:, :], pattern=[[1, SLOTS]], base=0, channel_multiplier=0,
                      allow_small_or_imprecise_dtypes=True).then_inc(consts, 1)
            pool.wait_ge(x_turned, 4)
            pool.dma_start(xn_rows[:, 0, :], b_out.partition_broadcast(P)).then_inc(b_out_in, 16)
            pool.wait_ge(mixed, 1)
            pool.wait_ge(lows, NH)
            pool.dma_start(bgu[:, :, :], b_gate_up_col).then_inc(late_in, 16)
            pool.dma_start(bdown_sb, b_down).then_inc(late_in, 16)
            pool.wait_ge(logits_ready, TT)
            pool.dma_start(gfin, g_final.partition_broadcast(P)).then_inc(gfin_in, 16)

        @block.scalar
        def _(a):
            for t in range(TT):
                a.dma_start(x_rows[:, t, :], x[t * P:(t + 1) * P, :]).then_inc(x_in, 16)
            for dst, src in ((c_sb, c_col), (ga_sb, g_attn_col), (gf_sb, g_ffn_col), (ba_sb, b_ada_col),
                             (bi_sb, b_in_col), (sink_sb[:, :], sinks.partition_broadcast(P)),
                             (br_sb[:, :], b_router.partition_broadcast(P)),
                             (wr_sb[:, :, :], w_router.rearrange("(k p) n -> p k n", p=P))):
                a.dma_start(dst, src).then_inc(vec_in, 16)
            a.dma_start(table_sb[0:BUCKETS, :], rel_table).then_inc(hot_in, 16)
            a.dma_start(table_sb[BUCKETS:BUCKETS + 2, :], masks).then_inc(hot_in, 16)
            a.dma_start(hot_sb, bucket_hot).then_inc(hot_in, 16)
            for i, part in enumerate((GATE_A, GATE_F)):
                a.dma_start(gates[:, i, :], b_ada_row[part * D:(part + 1) * D].partition_broadcast(P)
                            ).then_inc(same_in, 16)
            for t in range(TT):
                a.dma_start(v_rows[:, t, 0:512], b_in_row[1024:1536].partition_broadcast(P)).then_inc(same_in, 16)
                a.dma_start(v_rows[:, t, 512:640], b_in_row[2176:2304].partition_broadcast(P)).then_inc(same_in, 16)

            a.wait_ge(vec_in, 16 * 8)
            a.activation(sc_sb, c_sb, ACT.Sigmoid).then_inc(sc_sig, 1)
            a.wait_ge(line_ready, 1)
            a.activation(line_sb, bank[7][0:NH, 0:384], ACT.Copy, scale=-1.0).then_inc(line_copied, 1)
            a.wait_ge(line_copied, 1)
            a.dma_start(toeplitz, line_sb).then_inc(line_out, 16)

            a.wait_ge(x_in, 16 * TT)
            for t in range(TT):
                a.activation(xn_rows[:, t, :], x_rows[:, t, :], ACT.Square,
                             accum_out=stat[:, t:t + 1]).then_inc(squares, 1)
            a.wait_ge(means, 1)
            a.activation(stat[:, 4:6], stat[:, 2:4], ACT.Sqrt).then_inc(roots, 1)

            a.wait_ge(line_out, 16)
            a.dma_start(bias[:, :, :], bass.AP(toeplitz.tensor, toeplitz.offset, [[1, P], [384, NH], [1, S]])
                        ).then_inc(bias_in, 16)

            a.wait_ge(mod_ready, 1)
            for k in range(KT):
                if k % 4 == 0:
                    a.wait_ge(x_turned, 3 + k // 4)
                last = a.activation(hT[:, k, P:2 * P], bank[2 + k // 4][:, (k % 4) * P:(k % 4 + 1) * P],
                                    ACT.Identity, bias=add_a[:, k:k + 1], scale=mul_a[:, k:k + 1])
            last.then_inc(hT_act, 1)

            for job, dst, blk, bias_col, n in ((0, qT, 0, 0, 2), (1, qT, 2, 2, 2), (2, kT, 0, 4, 2), (3, kT, 2, 6, 2),
                                               (6, qT, 4, 4, 2), (7, qT, 6, 6, 2), (8, kT, 4, 16, 1)):
                wait_job(a, job)
                for j in range(n):
                    b_sb = (nbq_sb if dst is qT else bi_sb)[:, bias_col + j:bias_col + j + 1]
                    to, frm = (ap.rearrange("p (t n) -> p t n", t=TT)
                               for ap in (dst[:, blk + j, :], bank[job % 4][:, j * S:(j + 1) * S]))
                    if dst is qT:
                        frm = frm[:, :, ::-1]
                    last = a.activation(to, frm, ACT.Identity,
                                        bias=b_sb, scale=-DH ** -0.5 if dst is qT else 1.0)
                last.then_inc(proj_act, 1)

            def exp_head(h):
                a.wait_ge(lows, h + 1)
                a.activation(prob[:, h % 2, 0:256], prob[:, h % 2, 0:256], ACT.Exp, bias=lowest[:, h, 1:2],
                             scale=-1.0, accum_out=rowsum[:, h, 1:2])
                if h >= NHM:
                    sink = head_of(h) - NHM
                    a.activation(sinkexp[:, h - NHM, :], lowest[:, h, :], ACT.Exp, bias=sink_sb[:, sink:sink + 1])
                a.activation(prob[:, h % 2, 256:384], prob[:, h % 2, 256:384], ACT.Exp, bias=lowest[:, h, 0:1],
                             scale=-1.0, accum_out=rowsum[:, h, 0:1]).then_inc(exps, 1)

            def take_pT(h):
                a.wait_ge(p_turned, h + 1)
                if h >= 2:
                    a.wait_ge(o_ready, h - 1)
                a.activation(probT[:, h % 2, :], bank[2 + h % 2][:, 0:384], ACT.Copy).then_inc(pT_ready, 1)

            for h in range(NH + 1):
                if h < NH:
                    exp_head(h)
                if h >= 1:
                    take_pT(h - 1)

            for t in range(TT):
                a.wait_ge(x1_ready, t + 1)
                a.activation(xn_rows[:, t, :], x_rows[:, t, :], ACT.Square,
                             accum_out=stat[:, 8 + t:9 + t]).then_inc(squares, 1)
                a.wait_ge(means, t + 2)
                a.activation(stat[:, 12 + t:13 + t], stat[:, 10 + t:11 + t], ACT.Sqrt).then_inc(roots, 1)
            for t in range(TT):
                a.wait_ge(x1_turned, 2 * t + 2)
                for k in range(4, KT):
                    last = a.activation(hT[:, k, t * P:(t + 1) * P], bank[5 + 2 * t][:, (k % 4) * P:(k % 4 + 1) * P],
                                        ACT.Identity, bias=add_f[:, k:k + 1], scale=mul_f[:, k:k + 1])
                last.then_inc(h2_act, 1)
            for t in range(TT):
                a.wait_ge(top_ready, t + 1)
                a.activation(combine[:, t, :], logit[:, t, 0:NE], ACT.Exp, bias=top_stat[:, t, 0:1]
                             ).then_inc(top_exp, 1)
            a.wait_ge(comb_turned, 1)
            a.activation(combT, bank[4][0:NE, 0:S], ACT.Copy).then_inc(combT_ready, 1)

            def take_y(half, it, u):
                a.wait_ge(y_turned, it * 4 + (2 * u + half + 1))
                if half == 0:
                    a.wait_ge(scattered, it * 2 + (u + 1))
                a.activation(y_rows[:, half * 512:(half + 1) * 512], bank[7][:, :], ACT.Copy).then_inc(y_ready, 1)

            def experts(it, p):
                for e in range(EPB):
                    u, odd = divmod(e, 2)

                    def sigmoid(c):
                        a.wait_ge(gate_cut, it * (2 * EPB) + (2 * e + c + 1))
                        a.activation(sig[:, c, :], gu[:, c, 0, :, :].rearrange("p m n -> p (m n)"), ACT.Sigmoid,
                                     scale=ALPHA).then_inc(sig_ready, 1)

                    sigmoid(0)
                    if odd:
                        a.wait_ge(g_turned, it * 2 + (u + 1))
                        a.wait_ge(scattered, it * 2 + (u + 2))
                        a.activation(gT, bank[6][:, 0:S], ACT.Copy).then_inc(gT_ready, 1)
                    else:
                        take_y(0, it, u)
                    sigmoid(1)
                    if not odd:
                        take_y(1, it, u)
                    wait_experts(a, it, e, 6)
                    a.activation(yT[:, :, odd * SLOTS:(odd + 1) * SLOTS],
                                 bank[7][:, :].rearrange("p (k n) -> p k n", k=KT), ACT.Copy).then_inc(yT_ready, 1)

            bodies = all_rounds(a, experts)
            for half in range(2):
                take_y(half, bodies, 0)
            for t in range(TT):
                a.wait_ge(x2_ready, t + 1)
                a.activation(xn_rows[:, t, :], x_rows[:, t, :], ACT.Square,
                             accum_out=stat[:, 8 + t:9 + t]).then_inc(squares, 1)
                a.wait_ge(means, t + 4)
                a.activation(stat[:, 12 + t:13 + t], stat[:, 10 + t:11 + t], ACT.Sqrt).then_inc(roots, 1)

        @block.vector
        def _(v):
            own = [0]

            def link(ins):
                own[0] += 1
                ins.then_inc(dve, 1)
                v.wait_ge(dve, own[0])

            v.wait_ge(vec_in, 16 * 8)
            v.tensor_scalar(nsink_sb[:, :], sink_sb[:, :], -1.0, None, ALU.mult)
            v.tensor_scalar(nbq_sb[:, 0:4], bi_sb[:, 0:4], -DH ** -0.5, None, ALU.mult)
            v.tensor_scalar(nbq_sb[:, 4:8], bi_sb[:, 12:16], -DH ** -0.5, None, ALU.mult)
            v.wait_ge(sc_sig, 1)
            v.tensor_tensor(sc_sb, c_sb, sc_sb, ALU.mult).then_inc(sc_ready, 1)

            v.wait_ge(squares, 2)
            v.tensor_scalar(stat[:, 2:4], stat[:, 0:2], 1.0 / D, EPS, ALU.mult, ALU.add).then_inc(means, 1)
            v.wait_ge(roots, 1)
            link(v.reciprocal(stat[:, 6:8], stat[:, 4:6]))
            for t in range(TT):
                v.tensor_scalar(xn_rows[:, t, :], x_rows[:, t, :], stat[:, 6 + t:7 + t], None, ALU.mult
                                ).then_inc(xn_ready, 1)

            v.wait_ge(chunk_used, len(ADA_PE))
            link(v.tensor_tensor(mul_a, bank[4][:, 0:8], ba_sb[:, SCALE_A * KT:(SCALE_A + 1) * KT], ALU.add))
            v.tensor_tensor(add_a, bank[4][:, 8:16], ba_sb[:, SHIFT_A * KT:(SHIFT_A + 1) * KT], ALU.add)
            v.scalar_tensor_tensor(mul_a, mul_a, 1.0, ga_sb, ALU.add, ALU.mult).then_inc(mod_ready, 1)
            v.wait_ge(mod_ready, 1)
            for half in range(2):
                v.wait_ge(x_turned, 1 + half)
                h0 = hT[:, 4 * half:4 * half + 4, 0:P]
                link(v.tensor_tensor(h0, bank[half][:, :].rearrange("p (k n) -> p k n", k=4),
                                     mul_a[:, 4 * half:4 * half + 4].unsqueeze(2).broadcast_to([P, 4, P]), ALU.mult))
                last = v.tensor_tensor(h0, h0, add_a[:, 4 * half:4 * half + 4].unsqueeze(2).broadcast_to([P, 4, P]),
                                       ALU.add)
            last.then_inc(hT_dve, 1)

            def ada_chunk(i):
                n = HEAD_CHUNKS.index(ADA_DVE[i])
                wait_chunk(v, n)
                acc, w = ada_acc[i % 2], ring[:, n % RING]
                if i >= 2:
                    v.wait_ge(chunk_used, chunk_no(ADA_DVE[i - 2]) + 1)
                if i == 0:
                    v.wait_ge(line_out, 16)
                if i == 1:
                    v.wait_ge(line_ready, 1)
                link(v.tensor_scalar(acc, w[:, 0, :], sc_sb[:, 0:1], None, ALU.mult))
                for k in range(1, KT - 1):
                    link(v.scalar_tensor_tensor(acc, w[:, k, :], sc_sb[:, k:k + 1], acc, ALU.mult, ALU.add))
                v.scalar_tensor_tensor(acc, w[:, KT - 1, :], sc_sb[:, KT - 1:KT], acc, ALU.mult, ALU.add
                                       ).then_inc(ada_rows, 1)

            def take_gate(i):
                v.wait_ge(chunk_used, chunk_no(ADA_DVE[i]) + 1)
                g = gates[:, i // 6, (i % 2) * CW:(i % 2 + 1) * CW]
                v.tensor_tensor(g, bank[5][:, :], g, ALU.add).then_inc(ada_taken, 1)

            def take_v(job):
                wait_job(v, job)
                if job == 9:
                    for t in range(TT):
                        last = v.tensor_tensor(v_rows[:, t, 512:640], bank[1][:, t * P:(t + 1) * P],
                                               v_rows[:, t, 512:640], ALU.add)
                else:
                    last = v.tensor_tensor(v_rows[:, job - 4, 0:512], bank[job % 4][:, :], v_rows[:, job - 4, 0:512],
                                           ALU.add)
                last.then_inc(proj_dve, 1)

            v.wait_ge(same_in, 16 * 6)
            ada_chunk(0)
            ada_chunk(1)
            take_gate(0)
            ada_chunk(2)
            take_gate(1)
            take_v(4)
            take_v(5)
            for i in (3, 4, 5, 6):
                ada_chunk(i)
            v.wait_ge(chunk_used, chunk_no(ADA_DVE[5]) + 1)
            v.tensor_tensor(add_f, bank[4][:, 16:24], ba_sb[:, SHIFT_F * KT:(SHIFT_F + 1) * KT], ALU.add)
            link(v.tensor_tensor(mul_f, bank[4][:, 24:32], ba_sb[:, SCALE_F * KT:(SCALE_F + 1) * KT], ALU.add))
            link(v.scalar_tensor_tensor(mul_f, mul_f, 1.0, gf_sb, ALU.add, ALU.mult))
            ada_chunk(7)
            take_gate(6)
            take_gate(7)
            take_v(9)
            v.wait_ge(b_out_in, 16)
            v.wait_ge(ada_taken, 4)
            link(v.tensor_tensor(xn_rows[:, 0, :], xn_rows[:, 0, :], gates[:, 0, :], ALU.mult))
            for t in range(TT):
                link(v.tensor_tensor(x_rows[:, t, :], x_rows[:, t, :], xn_rows[:, 0, :], ALU.add))

            def logits(h):
                v.wait_ge(scores, h + 1)
                if h >= 2:
                    v.wait_ge(p_turned, h - 1)
                hh = head_of(h)
                for t, lo, hi, b0 in ((1, 0, 256, 0), (0, 256, 384, P)):
                    start = BIG if h < NHM else nsink_sb[:, hh - NHM:hh - NHM + 1]
                    last = v.tensor_tensor_reduce(prob[:, h % 2, lo:hi], bank[h % 2][:, lo:hi],
                                                  bias[:, hh, b0:b0 + hi - lo], 1.0, start, ALU.add, ALU.min,
                                                  lowest[:, h, t:t + 1])
                last.then_inc(lows, 1)

            def normalise(h):
                v.wait_ge(exps, h + 1)
                if h >= NHM:
                    link(v.tensor_tensor(rowsum[:, h, :], rowsum[:, h, :], sinkexp[:, h - NHM, :], ALU.add))
                link(v.reciprocal(rowsum[:, h, :], rowsum[:, h, :]))
                v.tensor_scalar(prob[:, h % 2, 0:256], prob[:, h % 2, 0:256], rowsum[:, h, 1:2], None, ALU.mult)
                v.tensor_scalar(prob[:, h % 2, 256:384], prob[:, h % 2, 256:384], rowsum[:, h, 0:1], None, ALU.mult
                                ).then_inc(probs_ready, 1)

            def take_o(blk):
                v.wait_ge(o_ready, 2 * blk + 2)
                to, frm = (ap.rearrange("p (t n) -> p t n", t=TT) for ap in (hT[:, blk, :], bank[6 + blk % 2][:, 0:S]))
                v.tensor_copy(to, frm[:, :, ::-1]).then_inc(o_taken, 1)

            v.wait_ge(bias_in, 16)
            for h in range(NH + 3):
                if h < NH:
                    logits(h)
                if 1 <= h <= NH:
                    normalise(h - 1)
                if h >= 4 and h % 2 == 0:
                    take_o(h // 2 - 2)

            for n, (half, t) in enumerate(((0, 0), (0, 1), (1, 0), (1, 1))):
                if t == 0:
                    v.wait_ge(mixed, half + 1)
                else:
                    v.wait_ge(chunk_used, PRE - 1 + half)
                cols = slice(half * 512, (half + 1) * 512)
                link(v.tensor_tensor(xn_rows[:, t, cols], bank[2 * t + half][:, :], gates[:, 0, cols], ALU.mult))
                add = v.tensor_tensor(x_rows[:, t, cols], x_rows[:, t, cols], xn_rows[:, t, cols], ALU.add)
                if half:
                    add.then_inc(x1_ready, 1)
            v.memset(yT, 0.0).then_inc(yT_ready, 1)
            v.memset(gT, 0.0).then_inc(gT_ready, 1)
            v.memset(logit[:, :, NE:NE + 4], BIG)
            v.memset(slot_of[:, :, ROUNDS * NE:], -1.0)
            link(v.memset(weight_of[:, :, ROUNDS * NE:], 0.0))
            for t in range(TT):
                v.wait_ge(squares, 3 + t)
                v.tensor_scalar(stat[:, 10 + t:11 + t], stat[:, 8 + t:9 + t], 1.0 / D, EPS, ALU.mult, ALU.add
                                ).then_inc(means, 1)
                v.wait_ge(roots, 2 + t)
                link(v.reciprocal(stat[:, 14 + t:15 + t], stat[:, 12 + t:13 + t]))
                v.tensor_scalar(xn_rows[:, t, :], x_rows[:, t, :], stat[:, 14 + t:15 + t], None, ALU.mult
                                ).then_inc(xn1_ready, 1)
            for t in range(TT):
                v.wait_ge(x1_turned, 2 * t + 1)
                h0 = hT[:, 0:4, t * P:(t + 1) * P]
                link(v.tensor_tensor(h0, bank[4 + 2 * t][:, :].rearrange("p (k n) -> p k n", k=4),
                                     mul_f[:, 0:4].unsqueeze(2).broadcast_to([P, 4, P]), ALU.mult))
                v.tensor_tensor(h0, h0, add_f[:, 0:4].unsqueeze(2).broadcast_to([P, 4, P]), ALU.add
                                ).then_inc(h2_dve, 1)

            for t in range(TT):
                v.wait_ge(logits_ready, t + 1)
                link(v.tensor_tensor(logit[:, t, 0:NE], bank[t][:, 0:NE], br_sb[:, :], ALU.add))
                link(v.max(top8[:, t, :], logit[:, t, 0:NE]))
                v.tensor_scalar(top_stat[:, t, 0:1], top8[:, t, 0:1], -1.0, None, ALU.mult).then_inc(top_ready, 1)
                link(v.memset(top8[:, t, TOPK:8], BIG))
                link(v.match_replace(left[:, t, :], top8[:, t, :], logit[:, t, 0:NE + 4], -BIG))
                v.tensor_tensor(chosen[:, t, :], left[:, t, 0:NE], logit[:, t, 0:NE], ALU.is_lt
                                ).then_inc(chosen_ready, 1)
            v.wait_ge(chosen_ready, TT)
            for t in range(TT):
                v.wait_ge(top_exp, t + 1)
                link(v.tensor_tensor(combine[:, t, :], combine[:, t, :], chosen[:, t, :], ALU.mult))
                link(v.tensor_reduce(top_stat[:, t, 1:2], combine[:, t, :], AX.X, ALU.add))
                link(v.reciprocal(top_stat[:, t, 2:3], top_stat[:, t, 1:2]))
                v.tensor_scalar(combine[:, t, :], combine[:, t, :], top_stat[:, t, 2:3], None, ALU.mult
                                ).then_inc(comb_ready, 1)
            v.wait_ge(comb_ready, TT)
            for r in range(ROUNDS):
                v.tensor_copy(weight_of[:, :, r * NE:(r + 1) * NE], combine[:, :, :])
            v.wait_ge(places, 1)
            v.tensor_reduce(peak[0:1, 0:1], bank[3][0:1, 0:NE], AX.X, ALU.max)
            first = slot_of[:, :, 0:NE]
            link(v.scalar_tensor_tensor(first, bank[2][:, 0:TT * NE].rearrange("p (t e) -> p t e", t=TT), 2.0 * S,
                                        chosen[:, :, :], ALU.add, ALU.mult))
            link(v.tensor_scalar(first, first, 2.0 * S, None, ALU.subtract))
            for r in range(1, ROUNDS):
                last = v.tensor_scalar(slot_of[:, :, r * NE:(r + 1) * NE], first, float(r * SLOTS), None, ALU.subtract)
            last.then_inc(routed, 1)
            v.wait_ge(routed, 1)

            def one_hots(b, pair, half, at):
                for t in range(TT):
                    v.tensor_scalar(pick[:, b, t, :], slot_no[:, :], slot_of[:, t, bass.ds(at, 1)], None, ALU.is_equal)
                    last = v.tensor_scalar(put[:, pair, t, half * SLOTS:(half + 1) * SLOTS], slot_no[:, :],
                                           slot_of[:, t, bass.ds(at, 1)], weight_of[:, t, bass.ds(at, 1)],
                                           ALU.is_equal, ALU.mult)
                last.then_inc(picks, 1)

            def take_xT(b, own_count):
                link_mul = v.tensor_tensor(xT_e[:, b], bank[6][:, :].rearrange("p (k n) -> p k n", k=KT),
                                           mul_f.unsqueeze(2).broadcast_to([P, KT, SLOTS]), ALU.mult)
                link_mul.then_inc(dve_e, 1)
                v.wait_ge(dve_e, own_count)
                v.tensor_tensor(xT_e[:, b], xT_e[:, b], add_f.unsqueeze(2).broadcast_to([P, KT, SLOTS]), ALU.add
                                ).then_inc(xT_ready, 1)

            def experts(it, p):
                for e in range(EPB):
                    done = it * (EPB * DVE_E)
                    nxt = e + 1
                    one_hots(nxt % 2, (nxt // 2) % 2, nxt % 2, it * EPB + nxt)
                    for c in range(2):
                        wait_experts(v, it, e, 2 * c + 2)
                        b_e = bgu[:, bass.ds(p * EPB + e, 1), :].rearrange("p a (g h m) -> p (a g) h m", g=2, h=2)
                        v.tensor_tensor(gu[:, c], bank[4 + c][:, :].rearrange("p (g m n) -> p g m n", g=2, m=HB),
                                        b_e[:, :, c, :].unsqueeze(3).broadcast_to([P, 2, HB, SLOTS]), ALU.add
                                        ).then_inc(gu_taken, 1)
                        v.wait_ge(gu_taken, it * (2 * EPB) + (2 * e + c + 1))
                        g, up = (gu[:, c, i, :, :].rearrange("p m n -> p (m n)") for i in (0, 1))
                        v.tensor_scalar(g, g, LIMIT, None, ALU.min).then_inc(gate_cut, 1)
                        v.tensor_scalar(up, up, LIMIT, -LIMIT, ALU.min, ALU.max).then_inc(dve_e, 1)
                        v.wait_ge(dve_e, done + (1 + DVE_E * e + 2 * c + 1))
                        v.scalar_tensor_tensor(up, up, 1.0, g, ALU.add, ALU.mult).then_inc(dve_e, 1)
                        v.wait_ge(dve_e, done + (1 + DVE_E * e + 2 * c + 2))
                        v.wait_ge(sig_ready, it * (2 * EPB) + (2 * e + c + 1))
                        v.tensor_tensor(act[:, c * HB:(c + 1) * HB, :].rearrange("p m n -> p (m n)"), up, sig[:, c, :],
                                        ALU.mult).then_inc(act_ready, 1)
                    v.wait_ge(gathered, it * EPB + (e + 2))
                    take_xT(nxt % 2, done + (1 + DVE_E * (e + 1)))

            v.wait_ge(late_in, 32)
            one_hots(0, 0, 0, 0)
            v.wait_ge(gathered, 1)
            take_xT(0, 1)
            all_rounds(v, experts)

            v.wait_ge(moe_done, 1)
            v.wait_ge(gfin_in, 16)
            for t in range(TT):
                for half in range(2):
                    cols = slice(half * 512, (half + 1) * 512)
                    link(v.tensor_tensor(xn_rows[:, t, cols], bank[2 * t + half][:, :], gates[:, 1, cols], ALU.mult))
                    add = v.tensor_tensor(x_rows[:, t, cols], x_rows[:, t, cols], xn_rows[:, t, cols], ALU.add)
                add.then_inc(x2_ready, 1)
            for t in range(TT):
                v.wait_ge(squares, 5 + t)
                v.tensor_scalar(stat[:, 10 + t:11 + t], stat[:, 8 + t:9 + t], 1.0 / D, EPS, ALU.mult, ALU.add
                                ).then_inc(means, 1)
                v.wait_ge(roots, 4 + t)
                link(v.reciprocal(stat[:, 14 + t:15 + t], stat[:, 12 + t:13 + t]))
                v.scalar_tensor_tensor(xn_rows[:, t, :], x_rows[:, t, :], stat[:, 14 + t:15 + t], gfin,
                                       ALU.mult, ALU.mult).then_inc(fin_ready, 1)

        @block.tensor
        def _(pe):
            pe.wait_ge(hot_in, 48)
            pe.matmul(bank[7][0:NH, 0:384], table_sb[:, :], hot_sb, start=True, stop=True).then_inc(line_ready, 1)
            pe.wait_ge(consts, 4)
            for t in range(TT):
                pe.wait_ge(xn_ready, t + 1)
                for half in range(2):
                    for j in range(4):
                        k = 4 * half + j
                        last = pe.transpose(bank[2 * t + half][:, j * P:(j + 1) * P], xn_rows[:, t, k * P:(k + 1) * P],
                                            ident[:, :])
                    last.then_inc(x_turned, 1)

            n = 0
            pe.wait_ge(sc_ready, 1)
            for part in range(2):
                for half in range(2):
                    wait_chunk(pe, n)
                    for m in range(HB):
                        at = part * 8 + half * 4 + m
                        for k in range(KT):
                            last = pe.matmul(bank[4][:, at:at + 1], ring[:, n % RING, k, m * P:(m + 1) * P],
                                             sc_sb[:, k:k + 1], start=(k == 0), stop=(k == KT - 1))
                    last.then_inc(chunk_used, 1)
                    n += 1

            job = 0
            summed = 0

            def free_bank(job):
                if job >= 4:
                    before = job - 4
                    if before in (4, 5):
                        pe.wait_ge(proj_dve, before - 3)
                    else:
                        pe.wait_ge(proj_act, before + 1 if before < 4 else before - 1)

            def columns(n, blocks, job):
                for b0 in range(0, len(blocks), 2):
                    free_bank(job)
                    for j, w_of in enumerate(blocks[b0:b0 + 2]):
                        for k in range(KT):
                            last = pe.matmul(bank[job % 4][:, j * S:(j + 1) * S], w_of(k), hT[:, k, :],
                                             start=(k == 0), stop=(k == KT - 1))
                    last.then_inc(*job_signal(job))
                    job += 1
                return job

            def ada_total(i):
                pe.wait_ge(ada_rows, i + 1)
                if i in (0, 1, 6, 7):
                    if i != 0:
                        pe.wait_ge(ada_taken, {1: 1, 6: 2, 7: 3}[i])
                    pe.matmul(bank[5][:, :], ones[:, :], ada_acc[i % 2], start=True, stop=True).then_inc(chunk_used, 1)
                else:
                    for m in range(HB):
                        at = 16 + (i - 2) * 4 + m
                        last = pe.matmul(bank[4][:, at:at + 1], ada_acc[i % 2][:, m * P:(m + 1) * P], ones[:, 0:1],
                                         start=True, stop=True)
                    last.then_inc(chunk_used, 1)

            pe.wait_ge(hT_dve, 1)
            pe.wait_ge(hT_act, 1)
            for kind in HEAD_CHUNKS[n:PRE - 2]:
                slot = ring[:, n % RING]
                if kind in ADA_DVE:
                    ada_total(ADA_DVE.index(kind))
                    n += 1
                    continue
                wait_chunk(pe, n)
                if kind in (Q_M, K_M, Q_S):
                    job = columns(n, [lambda k, m=m: slot[:, k, m * P:(m + 1) * P] for m in range(HB)], job)
                elif kind == V_M:
                    for t in range(TT):
                        free_bank(job)
                        for k in range(KT):
                            last = pe.matmul(bank[job % 4][:, :], hT[:, k, t * P:(t + 1) * P], slot[:, k, :],
                                             start=(k == 0), stop=(k == KT - 1))
                        last.then_inc(*job_signal(job))
                        job += 1
                else:
                    job = columns(n, [lambda k: slot[:, k, 0:P]], job)
                    free_bank(job)
                    for t in range(TT):
                        for k in range(KT):
                            last = pe.matmul(bank[job % 4][:, t * P:(t + 1) * P], hT[:, k, t * P:(t + 1) * P],
                                             slot[:, k, P:2 * P], start=(k == 0), stop=(k == KT - 1))
                    last.then_inc(*job_signal(job))
                    job += 1
                n += 1

            def score(h):
                if h >= 2:
                    pe.wait_ge(lows, h - 1)
                rows = slice(DH * (h % 2), DH * (h % 2) + DH)
                kb = h // 2 if h < NHM else 4
                pe.matmul(bank[h % 2][:, 0:256], qT[rows, h // 2, P:2 * P], kT[rows, kb, :], start=True, stop=True)
                pe.matmul(bank[h % 2][:, 256:384], qT[rows, h // 2, 0:P], kT[rows, kb, 0:P], start=True, stop=True
                          ).then_inc(scores, 1)

            def turn_p(h):
                pe.wait_ge(probs_ready, h + 1)
                if h >= 2:
                    pe.wait_ge(pT_ready, h - 1)
                for to, frm in ((0, 256), (128, 0), (256, 128)):
                    last = pe.transpose(bank[2 + h % 2][:, to:to + P], prob[:, h % 2, frm:frm + P], ident[:, :])
                last.then_inc(p_turned, 1)

            def values(h):
                pe.wait_ge(pT_ready, h + 1)
                blk, half = divmod(h, 2)
                if half == 0 and blk >= 2:
                    pe.wait_ge(o_taken, blk - 1)
                o = bank[6 + blk % 2][DH * half:DH * half + DH, 0:S]
                v0 = h * DH if h < NHM else 512 + half * DH
                pe.matmul(o, v_rows[:, 0, v0:v0 + DH], probT[:, h % 2, 0:256], start=True, stop=False)
                pe.matmul(o[:, P:2 * P], v_rows[:, 1, v0:v0 + DH], probT[:, h % 2, 256:384], start=False, stop=True
                          ).then_inc(o_ready, 1)

            pe.wait_ge(proj_act, 7)
            pe.wait_ge(proj_dve, 3)
            for h in range(NH + 2):
                if h < NH:
                    score(h)
                if 1 <= h <= NH:
                    turn_p(h - 1)
                if h >= 2:
                    values(h - 2)

            pe.wait_ge(o_taken, NHM)
            for half in range(2):
                wait_chunk(pe, n)
                for t in range(TT):
                    for k in range(KT):
                        last = pe.matmul(bank[2 * t + half][:, :], hT[:, k, t * P:(t + 1) * P],
                                         ring[:, n % RING, k, :], start=(k == 0), stop=(k == KT - 1))
                    last.then_inc(mixed if t == 0 else chunk_used, 1)
                n += 1
            assert n == PRE
            for t in range(TT):
                pe.wait_ge(xn1_ready, t + 1)
                for half in range(2):
                    for j in range(4):
                        k = 4 * half + j
                        last = pe.transpose(bank[4 + 2 * t + half][:, j * P:(j + 1) * P],
                                            xn_rows[:, t, k * P:(k + 1) * P], ident[:, :])
                    last.then_inc(x1_turned, 1)
            for t in range(TT):
                pe.wait_ge(h2_dve, t + 1)
                pe.wait_ge(h2_act, t + 1)
                for k in range(KT):
                    last = pe.matmul(bank[t][:, 0:NE], hT[:, k, t * P:(t + 1) * P], wr_sb[:, k, :],
                                     start=(k == 0), stop=(k == KT - 1))
                last.then_inc(logits_ready, 1)
            pe.wait_ge(chosen_ready, TT)
            pe.matmul(bank[2][:, 0:NE], earlier[:, :], chosen[:, 0, :], start=True, stop=True)
            pe.matmul(bank[2][:, NE:2 * NE], ones[:, :], chosen[:, 0, :], start=True, stop=False)
            pe.matmul(bank[2][:, NE:2 * NE], earlier[:, :], chosen[:, 1, :], start=False, stop=True)
            pe.matmul(bank[3][:, 0:NE], ones[:, :], chosen[:, 0, :], start=True, stop=False)
            pe.matmul(bank[3][:, 0:NE], ones[:, :], chosen[:, 1, :], start=False, stop=True).then_inc(places, 1)
            pe.wait_ge(comb_ready, TT)
            for t in range(TT):
                last = pe.transpose(bank[4][0:NE, t * P:(t + 1) * P], combine[:, t, :], ident[:, :])
            last.then_inc(comb_turned, 1)

            total = [[bank[2 * t + half] for half in range(2)] for t in range(TT)]
            pe.wait_ge(combT_ready, 1)
            pe.wait_ge(late_in, 32)
            pe.wait_ge(routed, 1)
            for t in range(TT):
                for half in range(2):
                    last = pe.matmul(total[t][half][:, :], combT[:, t * P:(t + 1) * P],
                                     bdown_sb[:, half * 512:(half + 1) * 512], start=True, stop=False)
            last.then_inc(scattered, 1)

            def gather(b):
                for k in range(KT):
                    for t in range(TT):
                        last = pe.matmul(bank[6][:, k * SLOTS:(k + 1) * SLOTS], xn_rows[:, t, k * P:(k + 1) * P],
                                         pick[:, b, t, :], start=(t == 0), stop=(t == TT - 1))
                last.then_inc(gathered, 1)

            def turn_y(half):
                for j in range(4):
                    last = pe.transpose(bank[7][:, j * P:(j + 1) * P], yT[:, 4 * half + j, :], ident[:, :])
                last.then_inc(y_turned, 1)

            def scatter(stop, signal):
                for t in range(TT):
                    for half in range(2):
                        last = pe.matmul(total[t][half][:, :], gT[:, t * P:(t + 1) * P],
                                         y_rows[:, half * 512:(half + 1) * 512], start=False, stop=stop)
                last.then_inc(signal, 1)

            def experts(it, p):
                for e in range(EPB):
                    u, odd = divmod(e, 2)
                    b = e % 2
                    first = PRE + CPE * e

                    def gate_up(c):
                        for g in range(2):
                            n = first + 2 * c + g
                            wait_chunk(pe, n, it)
                            for m in range(HB):
                                at = (g * HB + m) * SLOTS
                                for k in range(KT):
                                    last = pe.matmul(bank[4 + c][:, at:at + SLOTS],
                                                     ring[:, n % RING, k, m * P:(m + 1) * P], xT_e[:, b, k, :],
                                                     start=(k == 0), stop=(k == KT - 1))
                            last.then_inc(chunk_used, 1)

                    pe.wait_ge(xT_ready, it * EPB + (e + 1))
                    gate_up(0)
                    if odd:
                        for t in range(TT):
                            last = pe.transpose(bank[6][:, t * P:(t + 1) * P], put[:, u % 2, t, :], ident[:, :])
                        last.then_inc(g_turned, 1)
                    else:
                        pe.wait_ge(yT_ready, it * EPB + (e + 1))
                        turn_y(0)
                    gate_up(1)
                    if not odd:
                        pe.wait_ge(y_ready, it * 4 + (2 * u + 1))
                        turn_y(1)
                    pe.wait_ge(picks, it * EPB + (e + 2))
                    if odd:
                        pe.wait_ge(gT_ready, it * 2 + (u + 2))
                    gather(1 - b)
                    if not odd:
                        pe.wait_ge(y_ready, it * 4 + (2 * u + 2))
                        pe.wait_ge(gT_ready, it * 2 + (u + 1))
                        scatter(False, scattered)
                    else:
                        pe.wait_ge(yT_ready, it * EPB + (e + 1))
                    pe.wait_ge(act_ready, it * (2 * EPB) + (2 * e + 2))
                    for c in range(2):
                        n = first + 4 + c
                        wait_chunk(pe, n, it)
                        for m in range(HB):
                            at = (c * HB + m) * SLOTS
                            for k in range(KT):
                                last = pe.matmul(bank[7][:, at:at + SLOTS], ring[:, n % RING, k, m * P:(m + 1) * P],
                                                 act[:, k, :], start=(k == 0), stop=(k == KT - 1))
                        last.then_inc(chunk_used, 1)

            pe.wait_ge(picks, 1)
            gather(0)
            bodies = all_rounds(pe, experts)
            pe.wait_ge(yT_ready, bodies * EPB + 1)
            turn_y(0)
            pe.wait_ge(y_ready, bodies * 4 + 1)
            turn_y(1)
            pe.wait_ge(y_ready, bodies * 4 + 2)
            pe.wait_ge(gT_ready, bodies * 2 + 1)
            scatter(True, moe_done)


def kernel(x, c, g_attn, w_ada, b_ada, w_in, b_in, w_out, b_out, rel_table, sinks, g_ffn, w_router, b_router,
           w_gate_up, b_gate_up, w_down, b_down, g_final):
    import concourse.bacc as bacc
    from concourse.bass_utils import run_bass_kernel_spmd

    def columns(a, tiles):
        return np.ascontiguousarray(np.asarray(a).reshape(tiles, P).T)

    b_in_0 = np.asarray(b_in)[0]
    swa_q = b_in_0[1536:2048].reshape(2, 4, DH).transpose(1, 0, 2).reshape(-1)
    b_in_blocks = np.concatenate([b_in_0[:1536], swa_q, b_in_0[2048:]])
    w_q = np.asarray(w_in)[0]
    w_q = np.concatenate([w_q[:, :1536], w_q[:, 1536:2048].reshape(D, 2, 4, DH).transpose(0, 2, 1, 3).reshape(D, 512),
                          w_q[:, 2048:]], axis=1)
    w_o = np.asarray(w_out)[0]
    w_o = np.concatenate([w_o[:512], w_o[512:].reshape(2, 4, DH, D).transpose(1, 0, 2, 3).reshape(512, D)])

    arrays = {
        "x": np.asarray(x)[0], "c_col": columns(c, KT), "g_attn_col": columns(g_attn, KT),
        "w_ada": np.asarray(w_ada)[0], "b_ada_col": columns(b_ada, 6 * KT), "b_ada_row": np.asarray(b_ada)[0],
        "w_in": w_q, "b_in_col": columns(b_in_blocks, D_IN // P), "b_in_row": b_in_0,
        "w_out": w_o, "b_out": np.asarray(b_out)[0], "rel_table": np.asarray(rel_table), "sinks": np.asarray(sinks)[0],
        "g_ffn_col": columns(g_ffn, KT), "w_router": np.asarray(w_router)[0], "b_router": np.asarray(b_router)[0],
        "w_gate_up": np.asarray(w_gate_up)[0],
        "b_gate_up_col": np.ascontiguousarray(np.asarray(b_gate_up)[0].reshape(NE, 16, P).transpose(2, 0, 1)),
        "w_down": np.asarray(w_down)[0], "b_down": np.asarray(b_down)[0], "g_final": np.asarray(g_final),
        "bucket_hot": bucket_table(), "masks": mask_rows(),
    }
    arrays = {name: np.ascontiguousarray(a) for name, a in arrays.items()}
    nc = bacc.Bacc("TRN2", target_bir_lowering=False, num_devices=1)
    args = {name: nc.dram_tensor(name, a.shape, mybir.dt.from_np(a.dtype), kind="ExternalInput").ap()
            for name, a in arrays.items()}
    toeplitz = nc.dram_tensor("bias_lines", [NH, 384], F32, kind="Internal").ap()
    out = nc.dram_tensor("out", [S, D], F32, kind="ExternalOutput").ap()
    build(nc, **args, toeplitz=toeplitz, out=out)
    result = run_bass_kernel_spmd(nc, [arrays], core_ids=[0])
    return result.results[0]["out"].reshape(1, S, D)
```

```python
from contextlib import ExitStack
import math

import concourse.bass as bass
from concourse import mybir
import numpy as np

P = 128
D = 1024
S = 256
TT = S // P
KT = D // P
DH = 64
NH = 16
NHM = 8
QK_COLS = 512
D_IN = 2304
NE = 32
TOPK = 4
FF = 1024
LIMIT = 7.0
ALPHA = 1.702
EPS = 1e-5
NEG = -1e30
BIG = 3.0e38
BUCKETS = 32
MAX_DIST = 1024
WINDOW = 128

SLOTS = 64
PB = 4
ROUNDS = S // SLOTS
RING = 8
CW = 512
EPB = 4
CPE = 6
ITERS = NE // EPB
HB = 4
QW = CW // 2

F32 = mybir.dt.float32
I32 = mybir.dt.int32
ALU = mybir.AluOpType
ACT = mybir.ActivationFunctionType
AX = mybir.AxisListType

SHIFT_A, SCALE_A, GATE_A, SHIFT_F, SCALE_F, GATE_F = range(6)
ADA = [("ada", part * D + half * CW) for part in (SCALE_A, SHIFT_A, GATE_A, SHIFT_F, SCALE_F, GATE_F) for half in (0, 1)]
GATE_CHUNKS = [i for i, (_, first) in enumerate(ADA) if first // D in (GATE_A, GATE_F)]
Q_M, K_M, V_M, Q_S, KV_S = [("in", CW * i) for i in range(5)]
HEAD_CHUNKS = ADA[0:4] + [Q_M, K_M, ADA[4], V_M, ADA[5], ADA[6], Q_S, ADA[7], ADA[8], KV_S,
                          ADA[9], ADA[10], ADA[11], ("out", 0), ("out", CW)]
PRE = len(HEAD_CHUNKS)


def bucket_table():
    hot = np.zeros((BUCKETS + 2, 384), np.float32)
    exact = BUCKETS // 2
    for m in range(384):
        d = 255 - m
        if d >= 0:
            if d < exact:
                b = d
            else:
                nf = np.float32(d) / np.float32(exact)
                b = exact + int(np.float32(np.log(nf)) / np.float32(math.log(MAX_DIST / exact)) * np.float32(BUCKETS - exact))
                b = min(b, BUCKETS - 1)
            hot[b, m] = 1.0
        hot[BUCKETS, m] = d < 0
        hot[BUCKETS + 1, m] = d < 0 or d >= WINDOW
    return hot


def mask_rows():
    rows = np.zeros((2, NH), np.float32)
    rows[0, :NHM] = NEG
    rows[1, NHM:] = NEG
    return rows


def build(nc, x, vectors, w_ada, b_ada_row, w_in, b_in_row, w_out, b_out, rel_table,
          sinks, w_router, b_router, w_gate_up, b_gate_up, w_down, b_down, g_final, bucket_hot, masks,
          toeplitz, out):
    with ExitStack() as ctx:
        def sb(name, shape, dt=F32):
            return ctx.enter_context(nc.sbuf_tensor(name, shape, dt))

        def sem(name):
            return ctx.enter_context(nc.semaphore(name))

        bank = [ctx.enter_context(nc.psum_tensor(f"bank{i}", [P, 512], F32)) for i in range(8)]

        ring = sb("ring", [P, RING, KT, CW])
        x_rows = sb("x_rows", [P, TT, D])
        xn_rows = sb("xn_rows", [P, TT, D])
        hT = sb("hT", [P, KT, S])
        gates = sb("gates", [P, 2, D])
        ident = sb("ident", [P, P])
        ones = sb("ones", [P, P])
        earlier = sb("earlier", [P, P])
        slot_no = sb("slot_no", [P, SLOTS])
        col = sb("col", [P, 160])
        VECS = 90
        c_sb, ga_sb, gf_sb = col[:, 0:8], col[:, 8:16], col[:, 16:24]
        ba_sb, bi_sb = col[:, 24:72], col[:, 72:90]
        sc_sb = col[:, 90:98]
        nbq_sb = col[:, 98:106]
        mul_a, add_a = col[:, 106:114], col[:, 114:122]
        mul_f, add_f = col[:, 122:130], col[:, 130:138]
        stat = sb("stat", [P, 16])
        sink_sb = sb("sink_sb", [P, NHM])
        nsink_sb = sb("nsink_sb", [P, NHM])
        table_sb = sb("table_sb", [BUCKETS + 2, NH])
        wr_sb = sb("wr_sb", [P, KT, NE])
        br_sb = sb("br_sb", [P, NE])
        lowest = sb("lowest", [P, NH, TT])
        rowsum = sb("rowsum", [P, NH, TT])
        sinkexp = sb("sinkexp", [P, NHM, TT])
        peak = sb("peak", [1, 2], I32)
        prob = sb("prob", [P, PB, 384])
        probT = sb("probT", [P, 2, 384])
        prob_flat = prob[:, :, :].rearrange("p a n -> p (a n)")
        ada_acc = prob_flat[:, 0:CW], prob_flat[:, CW:2 * CW]
        hot_sb = probT[0:BUCKETS + 2, 0, :]
        line_sb = probT[0:NH, 1, :]
        late = sb("late", [P, 8704])
        bias = late[:, 0:4096].rearrange("p (h n) -> p h n", h=NH)
        qT = late[:, 4096:6144].rearrange("p (b n) -> p b n", b=8)
        kT = late[:, 6144:7424].rearrange("p (b n) -> p b n", b=5)
        v_rows = late[:, 7424:8704].rearrange("p (t n) -> p t n", t=TT)

        used = [0]

        def piece(n):
            used[0] += n
            return late[:, used[0] - n:used[0]]

        xT_e = piece(2 * KT * 2 * SLOTS).rearrange("p (b k n) -> p b k n", b=2, k=KT)
        gate, sig, up, act = piece(512), piece(512), piece(512), piece(512)
        actT = piece(512)
        y_rows = piece(2 * 512).rearrange("p (h n) -> p h n", h=2)
        gT = piece(TT * 2 * P).rearrange("p (t s n) -> p t s n", t=TT, s=2)
        is_expert = piece(2 * SLOTS).rearrange("p (b n) -> p b n", b=2)
        slot_of = piece(TT * (ROUNDS * NE + 2)).rearrange("p (t n) -> p t n", t=TT)
        weight_of = piece(TT * (ROUNDS * NE + 2)).rearrange("p (t n) -> p t n", t=TT)
        pick = piece(TT * 2 * SLOTS).rearrange("p (t n) -> p t n", t=TT)
        put = piece(TT * 3 * SLOTS).rearrange("p (t n) -> p t n", t=TT)
        route = piece(TT * 160).rearrange("p (t n) -> p t n", t=TT)
        combT = piece(S)[0:NE, :]
        assert used[0] <= 8704
        logit, left = route[:, :, 0:40], route[:, :, 40:76]
        top8, chosen, combine = route[:, :, 76:84], route[:, :, 84:116], route[:, :, 116:148]
        top_stat = route[:, :, 148:152]
        bdown_sb = gates[0:NE, 0, :]
        gfin = gates[:, 0, :]
        bgu = hT[:, :, :].rearrange("p k n -> p (k n)")

        chunk_in = [sem(f"chunk_in{i}") for i in range(RING)]
        chunk_used = sem("chunk_used")
        x_in, vec_in, same_in, hot_in = sem("x_in"), sem("vec_in"), sem("same_in"), sem("hot_in")
        line_out, bias_in, b_out_in = sem("line_out"), sem("bias_in"), sem("b_out_in")
        gfin_in, result_out, wr_in = sem("gfin_in"), sem("result_out"), sem("wr_in")
        consts, line_ready, line_copied = sem("consts"), sem("line_ready"), sem("line_copied")
        dve = sem("dve")
        squares, means, roots = sem("squares"), sem("means"), sem("roots")
        sc_sig, sc_ready = sem("sc_sig"), sem("sc_ready")
        xn_ready, x_turned, hT_dve, hT_act = sem("xn_ready"), sem("x_turned"), sem("hT_dve"), sem("hT_act")
        mod_ready, ada_rows, ada_taken = sem("mod_ready"), sem("ada_rows"), sem("ada_taken")
        proj, proj_act, proj_dve = sem("proj"), sem("proj_act"), sem("proj_dve")
        scores, lows, exps, probs_ready = sem("scores"), sem("lows"), sem("exps"), sem("probs_ready")
        p_turned, pT_ready, o_ready, o_taken = sem("p_turned"), sem("pT_ready"), sem("o_ready"), sem("o_taken")
        mixed, x1_ready, xn1_ready, x1_turned = sem("mixed"), sem("x1_ready"), sem("xn1_ready"), sem("x1_turned")
        h2_dve, h2_act, logits_ready, top_ready = sem("h2_dve"), sem("h2_act"), sem("logits_ready"), sem("top_ready")
        top_exp, chosen_ready, places = sem("top_exp"), sem("chosen_ready"), sem("places")
        comb_ready, comb_turned, combT_ready = sem("comb_ready"), sem("comb_turned"), sem("combT_ready")
        routed = sem("routed")
        bdown_in, bgu_in = sem("bdown_in"), sem("bgu_in")
        picks, gathered, xT_ready = sem("picks"), sem("gathered"), sem("xT_ready")
        gate_cut, is_ready = sem("gate_cut"), sem("is_ready")
        sig_ready, act_ready = sem("sig_ready"), sem("act_ready")
        dve_e = sem("dve_e")
        act_turned, actT_ready, y_ready = sem("act_turned"), sem("actT_ready"), sem("y_ready")
        g_turned, gT_ready, scattered = sem("g_turned"), sem("gT_ready"), sem("scattered")
        moe_done, x2_ready, fin_ready = sem("moe_done"), sem("x2_ready"), sem("fin_ready")

        block = ctx.enter_context(nc.Block())
        DVE_PAIR = 6
        G, U, T, Y = bank[4], bank[5], bank[6], bank[7]

        def wait_chunk(eng, n, it=None):
            landed = 16 * (n // RING + 1)
            eng.wait_ge(chunk_in[n % RING], landed if it is None else it * (16 * EPB * CPE // RING) + landed)

        def chunk_no(kind):
            return HEAD_CHUNKS.index(kind)

        JOB_CHUNK = [chunk_no(kind) for kind in (Q_M, K_M, V_M, Q_S, KV_S)]

        def job_signal(job):
            return (chunk_used if job % 2 else proj), 1

        def wait_job(eng, job):
            if job % 2:
                eng.wait_ge(chunk_used, JOB_CHUNK[job // 2] + 1)
            else:
                eng.wait_ge(proj, job // 2 + 1)

        def wait_experts(eng, it, e, chunks):
            eng.wait_ge(chunk_used, it * (EPB * CPE) + (PRE + CPE * e + chunks))

        def all_rounds(eng, body):
            with eng.Fori(0, ITERS) as p:
                body(p, p)
            eng.wait_ge(routed, 1)
            busiest = eng.value_load(peak[0:1, 0:1], min_val=1, max_val=S)
            with eng.If(busiest > SLOTS):
                with eng.Fori(1, (busiest + (SLOTS - 1)) // SLOTS) as r:
                    with eng.Fori(0, ITERS) as p:
                        body(r * ITERS + p, p)
            return (busiest + (SLOTS - 1)) // SLOTS * ITERS

        def head_of(h):
            return h if h < NHM else NHM + (h - NHM) // 2 + 4 * (h % 2)

        @block.sync
        def _(sp):
            for t in range(TT):
                sp.dma_start(x_rows[:, t, :], x[t * P:(t + 1) * P, :]).then_inc(x_in, 16)
            sp.dma_start(col[:, 0:VECS], vectors).then_inc(vec_in, 16)
            source = {"ada": w_ada, "in": w_in, "out": w_out}
            for n, (kind, first) in enumerate(HEAD_CHUNKS):
                if n >= RING:
                    sp.wait_ge(chunk_used, n - RING + 1)
                w = min(CW, source[kind].shape[1] - first)
                sp.dma_start(ring[:, n % RING, :, 0:w],
                             source[kind][:, first:first + w].rearrange("(k p) n -> p k n", p=P)
                             ).then_inc(chunk_in[n % RING], 16)

            def load_experts(it, p):
                for e in range(EPB):
                    for j in range(CPE):
                        n = PRE + CPE * e + j
                        sp.wait_ge(chunk_used, it * (EPB * CPE) + (n - RING + 1))
                        if j < 4:
                            src = w_gate_up[bass.ds(p * EPB + e, 1), :, j * CW:(j + 1) * CW]
                        else:
                            src = w_down[bass.ds(p * EPB + e, 1), :, (j - 4) * CW:(j - 3) * CW]
                        sp.dma_start(ring[:, n % RING], src.rearrange("a (k p) n -> p (a k) n", p=P)
                                     ).then_inc(chunk_in[n % RING], 16)

            all_rounds(sp, load_experts)
            for t in range(TT):
                sp.wait_ge(fin_ready, t + 1)
                sp.dma_start(out[t * P:(t + 1) * P, :], xn_rows[:, t, :]).then_inc(result_out, 16)
            sp.wait_ge(result_out, 16 * TT)

        @block.gpsimd
        def _(pool):
            pool.memset(ones[:, :], 1.0).then_inc(consts, 1)
            pool.wait_ge(consts, 1)
            pool.affine_select(out=ident[:, :], in_=ones[:, :], compare_op=ALU.is_equal, fill=0.0,
                               base=0, pattern=[[-1, P]], channel_multiplier=1).then_inc(consts, 1)
            pool.affine_select(out=earlier[:, :], in_=ones[:, :], compare_op=ALU.is_gt, fill=0.0,
                               base=0, pattern=[[1, P]], channel_multiplier=-1).then_inc(consts, 1)
            pool.iota(slot_no[:, :], pattern=[[1, SLOTS]], base=0, channel_multiplier=0,
                      allow_small_or_imprecise_dtypes=True).then_inc(consts, 1)
            pool.wait_ge(x_turned, 4)
            pool.dma_start(xn_rows[:, 0, :], b_out.partition_broadcast(P)).then_inc(b_out_in, 16)
            pool.wait_ge(x1_ready, TT)
            pool.dma_start(bdown_sb, b_down).then_inc(bdown_in, 16)
            pool.wait_ge(logits_ready, TT)
            pool.dma_start(bgu[0:NE, :], b_gate_up).then_inc(bgu_in, 16)
            pool.wait_ge(scattered, 1)
            pool.dma_start(gfin, g_final.partition_broadcast(P)).then_inc(gfin_in, 16)

        @block.scalar
        def _(a):
            a.dma_start(table_sb[0:BUCKETS, :], rel_table).then_inc(hot_in, 16)
            a.dma_start(table_sb[BUCKETS:BUCKETS + 2, :], masks).then_inc(hot_in, 16)
            a.dma_start(hot_sb, bucket_hot).then_inc(hot_in, 16)
            for i, part in enumerate((GATE_A, GATE_F)):
                a.dma_start(gates[:, i, :], b_ada_row[part * D:(part + 1) * D].partition_broadcast(P)
                            ).then_inc(same_in, 16)
            for t in range(TT):
                a.dma_start(v_rows[:, t, 0:512], b_in_row[1024:1536].partition_broadcast(P)).then_inc(same_in, 16)
                a.dma_start(v_rows[:, t, 512:640], b_in_row[2176:2304].partition_broadcast(P)).then_inc(same_in, 16)

            for dst, src in ((sink_sb[:, :], sinks.partition_broadcast(P)),
                             (br_sb[:, :], b_router.partition_broadcast(P)),
                             (wr_sb[:, :, :], w_router.rearrange("(k p) n -> p k n", p=P))):
                a.dma_start(dst, src).then_inc(wr_in, 16)

            a.wait_ge(vec_in, 16)
            a.activation(sc_sb, c_sb, ACT.Sigmoid).then_inc(sc_sig, 1)
            a.wait_ge(line_ready, 1)
            a.activation(line_sb, bank[7][0:NH, 0:384], ACT.Copy, scale=-1.0).then_inc(line_copied, 1)
            a.wait_ge(line_copied, 1)
            a.dma_start(toeplitz, line_sb).then_inc(line_out, 16)

            a.wait_ge(x_in, 16 * TT)
            for t in range(TT):
                a.activation(xn_rows[:, t, :], x_rows[:, t, :], ACT.Square,
                             accum_out=stat[:, t:t + 1]).then_inc(squares, 1)
            a.wait_ge(means, 1)
            a.activation(stat[:, 4:6], stat[:, 2:4], ACT.Sqrt).then_inc(roots, 1)

            a.wait_ge(line_out, 16)
            a.dma_start(bias[:, :, :], bass.AP(toeplitz.tensor, toeplitz.offset, [[1, P], [384, NH], [1, S]])
                        ).then_inc(bias_in, 16)

            a.wait_ge(mod_ready, 1)
            for k in range(KT):
                if k % 4 == 0:
                    a.wait_ge(x_turned, 3 + k // 4)
                last = a.activation(hT[:, k, P:2 * P], bank[2 + k // 4][:, (k % 4) * P:(k % 4 + 1) * P],
                                    ACT.Identity, bias=add_a[:, k:k + 1], scale=mul_a[:, k:k + 1])
            last.then_inc(hT_act, 1)

            for job, dst, blk, bias_col, n in ((0, qT, 0, 0, 2), (1, qT, 2, 2, 2), (2, kT, 0, 4, 2), (3, kT, 2, 6, 2),
                                               (6, qT, 4, 4, 2), (7, qT, 6, 6, 2), (8, kT, 4, 16, 1)):
                wait_job(a, job)
                for j in range(n):
                    b_sb = (nbq_sb if dst is qT else bi_sb)[:, bias_col + j:bias_col + j + 1]
                    to, frm = (ap.rearrange("p (t n) -> p t n", t=TT)
                               for ap in (dst[:, blk + j, :], bank[job % 4][:, j * S:(j + 1) * S]))
                    if dst is qT:
                        frm = frm[:, :, ::-1]
                    last = a.activation(to, frm, ACT.Identity,
                                        bias=b_sb, scale=-DH ** -0.5 if dst is qT else 1.0)
                last.then_inc(proj_act, 1)

            def exp_head(h):
                a.wait_ge(lows, h + 1)
                a.activation(prob[:, h % PB, 0:256], prob[:, h % PB, 0:256], ACT.Exp, bias=lowest[:, h, 1:2],
                             scale=-1.0, accum_out=rowsum[:, h, 1:2])
                if h >= NHM:
                    sink = head_of(h) - NHM
                    a.activation(sinkexp[:, h - NHM, :], lowest[:, h, :], ACT.Exp, bias=sink_sb[:, sink:sink + 1])
                a.activation(prob[:, h % PB, 256:384], prob[:, h % PB, 256:384], ACT.Exp, bias=lowest[:, h, 0:1],
                             scale=-1.0, accum_out=rowsum[:, h, 0:1]).then_inc(exps, 1)

            def take_pT(h):
                a.wait_ge(p_turned, h + 1)
                if h >= 2:
                    a.wait_ge(o_ready, h - 1)
                a.activation(probT[:, h % 2, :], bank[2 + h % 2][:, 0:384], ACT.Copy).then_inc(pT_ready, 1)

            a.wait_ge(wr_in, 16 * 3)
            for h in range(NH + 2):
                if h < NH:
                    exp_head(h)
                if h >= 2:
                    take_pT(h - 2)

            for t in range(TT):
                a.wait_ge(x1_ready, t + 1)
                a.activation(xn_rows[:, t, :], x_rows[:, t, :], ACT.Square,
                             accum_out=stat[:, 8 + t:9 + t]).then_inc(squares, 1)
                a.wait_ge(means, t + 2)
                a.activation(stat[:, 12 + t:13 + t], stat[:, 10 + t:11 + t], ACT.Sqrt).then_inc(roots, 1)
            for t in range(TT):
                a.wait_ge(x1_turned, 2 * t + 2)
                for k in range(4, KT):
                    last = a.activation(hT[:, k, t * P:(t + 1) * P], bank[5 + 2 * t][:, (k % 4) * P:(k % 4 + 1) * P],
                                        ACT.Identity, bias=add_f[:, k:k + 1], scale=mul_f[:, k:k + 1])
                last.then_inc(h2_act, 1)
            for t in range(TT):
                a.wait_ge(top_ready, t + 1)
                a.activation(combine[:, t, :], logit[:, t, 0:NE], ACT.Exp, bias=top_stat[:, t, 0:1]
                             ).then_inc(top_exp, 1)
            a.wait_ge(comb_turned, 1)
            a.activation(combT, bank[4][0:NE, 0:S], ACT.Copy).then_inc(combT_ready, 1)

            def experts(it, p):
                for e in range(EPB):
                    u, odd = divmod(e, 2)
                    a.wait_ge(gate_cut, it * EPB + (e + 1))
                    a.activation(sig, gate, ACT.Sigmoid, scale=ALPHA).then_inc(sig_ready, 1)
                    if not odd:
                        a.wait_ge(g_turned, it * 2 + (u + 1))
                        a.wait_ge(scattered, it * 2 + (u + 2))
                        a.activation(gT.rearrange("p t s n -> p (t s n)"), G[:, :], ACT.Copy).then_inc(gT_ready, 1)
                    a.wait_ge(act_turned, it * EPB + (e + 1))
                    a.activation(actT, T[:, :], ACT.Copy).then_inc(actT_ready, 1)
                    wait_experts(a, it, e, 6)
                    lo, hi = (y_rows[0:SLOTS, odd, :], Y[0:SLOTS, :]), (y_rows[SLOTS:P, 1 - odd, :], Y[SLOTS:P, :])
                    if not odd:
                        a.wait_ge(scattered, it * 2 + (u + 2))
                    a.activation(*lo, ACT.Copy)
                    a.activation(*hi, ACT.Copy).then_inc(y_ready, 1)

            all_rounds(a, experts)
            for t in range(TT):
                a.wait_ge(x2_ready, t + 1)
                a.activation(xn_rows[:, t, :], x_rows[:, t, :], ACT.Square,
                             accum_out=stat[:, 8 + t:9 + t]).then_inc(squares, 1)
                a.wait_ge(means, t + 4)
                a.activation(stat[:, 12 + t:13 + t], stat[:, 10 + t:11 + t], ACT.Sqrt).then_inc(roots, 1)

        @block.vector
        def _(v):
            own = [0]

            def link(ins):
                own[0] += 1
                ins.then_inc(dve, 1)
                v.wait_ge(dve, own[0])

            v.wait_ge(vec_in, 16)
            v.tensor_scalar(nbq_sb[:, 0:4], bi_sb[:, 0:4], -DH ** -0.5, None, ALU.mult)
            v.tensor_scalar(nbq_sb[:, 4:8], bi_sb[:, 12:16], -DH ** -0.5, None, ALU.mult)
            v.wait_ge(sc_sig, 1)
            v.tensor_tensor(sc_sb, c_sb, sc_sb, ALU.mult).then_inc(sc_ready, 1)

            v.wait_ge(squares, 2)
            v.tensor_scalar(stat[:, 2:4], stat[:, 0:2], 1.0 / D, EPS, ALU.mult, ALU.add).then_inc(means, 1)
            v.wait_ge(roots, 1)
            link(v.reciprocal(stat[:, 6:8], stat[:, 4:6]))
            for t in range(TT):
                v.tensor_scalar(xn_rows[:, t, :], x_rows[:, t, :], stat[:, 6 + t:7 + t], None, ALU.mult
                                ).then_inc(xn_ready, 1)

            def ada_chunk(i):
                n = chunk_no(ADA[i])
                wait_chunk(v, n)
                acc, w = ada_acc[i % 2], ring[:, n % RING]
                if i >= 2:
                    v.wait_ge(chunk_used, chunk_no(ADA[i - 2]) + 1)
                link(v.tensor_scalar(acc, w[:, 0, :], sc_sb[:, 0:1], None, ALU.mult))
                for k in range(1, KT - 1):
                    link(v.scalar_tensor_tensor(acc, w[:, k, :], sc_sb[:, k:k + 1], acc, ALU.mult, ALU.add))
                v.scalar_tensor_tensor(acc, w[:, KT - 1, :], sc_sb[:, KT - 1:KT], acc, ALU.mult, ALU.add
                                       ).then_inc(ada_rows, 1)

            v.wait_ge(sc_ready, 1)
            for i in range(4):
                ada_chunk(i)
            v.wait_ge(chunk_used, 4)
            link(v.tensor_tensor(mul_a, bank[4][:, 0:8], ba_sb[:, SCALE_A * KT:(SCALE_A + 1) * KT], ALU.add))
            v.tensor_tensor(add_a, bank[4][:, 8:16], ba_sb[:, SHIFT_A * KT:(SHIFT_A + 1) * KT], ALU.add)
            v.scalar_tensor_tensor(mul_a, mul_a, 1.0, ga_sb, ALU.add, ALU.mult).then_inc(mod_ready, 1)
            v.wait_ge(mod_ready, 1)
            for half in range(2):
                v.wait_ge(x_turned, 1 + half)
                h0 = hT[:, 4 * half:4 * half + 4, 0:P]
                link(v.tensor_tensor(h0, bank[half][:, :].rearrange("p (k n) -> p k n", k=4),
                                     mul_a[:, 4 * half:4 * half + 4].unsqueeze(2).broadcast_to([P, 4, P]), ALU.mult))
                last = v.tensor_tensor(h0, h0, add_a[:, 4 * half:4 * half + 4].unsqueeze(2).broadcast_to([P, 4, P]),
                                       ALU.add)
            last.then_inc(hT_dve, 1)

            def take_gate(i):
                v.wait_ge(chunk_used, chunk_no(ADA[i]) + 1)
                g = gates[:, i // 10, (i % 2) * CW:(i % 2 + 1) * CW]
                v.tensor_tensor(g, bank[5][:, :], g, ALU.add).then_inc(ada_taken, 1)

            def take_v(job):
                wait_job(v, job)
                if job == 9:
                    for t in range(TT):
                        last = v.tensor_tensor(v_rows[:, t, 512:640], bank[1][:, t * P:(t + 1) * P],
                                               v_rows[:, t, 512:640], ALU.add)
                else:
                    last = v.tensor_tensor(v_rows[:, job - 4, 0:512], bank[job % 4][:, :], v_rows[:, job - 4, 0:512],
                                           ALU.add)
                last.then_inc(proj_dve, 1)

            v.wait_ge(same_in, 16 * 6)
            ada_chunk(4)
            ada_chunk(5)
            take_gate(4)
            ada_chunk(6)
            take_gate(5)
            take_v(4)
            take_v(5)
            for i in (7, 8, 9, 10):
                ada_chunk(i)
            v.wait_ge(chunk_used, chunk_no(ADA[9]) + 1)
            v.tensor_tensor(add_f, bank[4][:, 16:24], ba_sb[:, SHIFT_F * KT:(SHIFT_F + 1) * KT], ALU.add)
            link(v.tensor_tensor(mul_f, bank[4][:, 24:32], ba_sb[:, SCALE_F * KT:(SCALE_F + 1) * KT], ALU.add))
            link(v.scalar_tensor_tensor(mul_f, mul_f, 1.0, gf_sb, ALU.add, ALU.mult))
            ada_chunk(11)
            take_gate(10)
            take_gate(11)
            take_v(9)
            v.wait_ge(b_out_in, 16)
            v.wait_ge(ada_taken, 4)
            link(v.tensor_tensor(xn_rows[:, 0, :], xn_rows[:, 0, :], gates[:, 0, :], ALU.mult))
            for t in range(TT):
                link(v.tensor_tensor(x_rows[:, t, :], x_rows[:, t, :], xn_rows[:, 0, :], ALU.add))

            def logits(h):
                v.wait_ge(scores, h + 1)
                if h >= PB:
                    v.wait_ge(p_turned, h - PB + 1)
                hh = head_of(h)
                for t, lo, hi, b0 in ((1, 0, 256, 0), (0, 256, 384, P)):
                    start = BIG if h < NHM else nsink_sb[:, hh - NHM:hh - NHM + 1]
                    last = v.tensor_tensor_reduce(prob[:, h % PB, lo:hi], bank[h % 2][:, lo:hi],
                                                  bias[:, hh, b0:b0 + hi - lo], 1.0, start, ALU.add, ALU.min,
                                                  lowest[:, h, t:t + 1])
                last.then_inc(lows, 1)

            def normalise(h):
                v.wait_ge(exps, h + 1)
                if h >= NHM:
                    link(v.tensor_tensor(rowsum[:, h, :], rowsum[:, h, :], sinkexp[:, h - NHM, :], ALU.add))
                link(v.reciprocal(rowsum[:, h, :], rowsum[:, h, :]))
                v.tensor_scalar(prob[:, h % PB, 0:256], prob[:, h % PB, 0:256], rowsum[:, h, 1:2], None, ALU.mult)
                v.tensor_scalar(prob[:, h % PB, 256:384], prob[:, h % PB, 256:384], rowsum[:, h, 0:1], None, ALU.mult
                                ).then_inc(probs_ready, 1)

            def take_o(blk):
                v.wait_ge(o_ready, 2 * blk + 2)
                to, frm = (ap.rearrange("p (t n) -> p t n", t=TT) for ap in (hT[:, blk, :], bank[6 + blk % 2][:, 0:S]))
                v.tensor_copy(to, frm[:, :, ::-1]).then_inc(o_taken, 1)

            v.wait_ge(bias_in, 16)
            v.wait_ge(wr_in, 16 * 3)
            link(v.tensor_scalar(nsink_sb[:, :], sink_sb[:, :], -1.0, None, ALU.mult))
            for h in range(NH + 4):
                if h < NH:
                    logits(h)
                if 1 <= h <= NH:
                    normalise(h - 1)
                if h >= 5 and h % 2 == 1:
                    take_o((h - 5) // 2)

            for n, (half, t) in enumerate(((0, 0), (0, 1), (1, 0), (1, 1))):
                if t == 0:
                    v.wait_ge(mixed, half + 1)
                else:
                    v.wait_ge(chunk_used, PRE - 1 + half)
                cols = slice(half * 512, (half + 1) * 512)
                link(v.tensor_tensor(xn_rows[:, t, cols], bank[2 * t + half][:, :], gates[:, 0, cols], ALU.mult))
                add = v.tensor_tensor(x_rows[:, t, cols], x_rows[:, t, cols], xn_rows[:, t, cols], ALU.add)
                if half:
                    add.then_inc(x1_ready, 1)
            v.memset(y_rows, 0.0).then_inc(y_ready, 1)
            v.memset(gT, 0.0).then_inc(gT_ready, 1)
            v.memset(logit[:, :, NE:NE + 4], BIG)
            v.memset(slot_of[:, :, ROUNDS * NE:], -1.0)
            link(v.memset(weight_of[:, :, ROUNDS * NE:], 0.0))
            for t in range(TT):
                v.wait_ge(squares, 3 + t)
                v.tensor_scalar(stat[:, 10 + t:11 + t], stat[:, 8 + t:9 + t], 1.0 / D, EPS, ALU.mult, ALU.add
                                ).then_inc(means, 1)
                v.wait_ge(roots, 2 + t)
                link(v.reciprocal(stat[:, 14 + t:15 + t], stat[:, 12 + t:13 + t]))
                v.tensor_scalar(xn_rows[:, t, :], x_rows[:, t, :], stat[:, 14 + t:15 + t], None, ALU.mult
                                ).then_inc(xn1_ready, 1)
            for t in range(TT):
                v.wait_ge(x1_turned, 2 * t + 1)
                h0 = hT[:, 0:4, t * P:(t + 1) * P]
                link(v.tensor_tensor(h0, bank[4 + 2 * t][:, :].rearrange("p (k n) -> p k n", k=4),
                                     mul_f[:, 0:4].unsqueeze(2).broadcast_to([P, 4, P]), ALU.mult))
                v.tensor_tensor(h0, h0, add_f[:, 0:4].unsqueeze(2).broadcast_to([P, 4, P]), ALU.add
                                ).then_inc(h2_dve, 1)

            for t in range(TT):
                v.wait_ge(logits_ready, t + 1)
                link(v.tensor_tensor(logit[:, t, 0:NE], bank[t][:, 0:NE], br_sb[:, :], ALU.add))
                link(v.max(top8[:, t, :], logit[:, t, 0:NE]))
                v.tensor_scalar(top_stat[:, t, 0:1], top8[:, t, 0:1], -1.0, None, ALU.mult).then_inc(top_ready, 1)
                link(v.memset(top8[:, t, TOPK:8], BIG))
                link(v.match_replace(left[:, t, :], top8[:, t, :], logit[:, t, 0:NE + 4], -BIG))
                v.tensor_tensor(chosen[:, t, :], left[:, t, 0:NE], logit[:, t, 0:NE], ALU.is_lt
                                ).then_inc(chosen_ready, 1)
            v.wait_ge(chosen_ready, TT)
            for t in range(TT):
                v.wait_ge(top_exp, t + 1)
                link(v.tensor_tensor(combine[:, t, :], combine[:, t, :], chosen[:, t, :], ALU.mult))
                link(v.tensor_reduce(top_stat[:, t, 1:2], combine[:, t, :], AX.X, ALU.add))
                link(v.reciprocal(top_stat[:, t, 2:3], top_stat[:, t, 1:2]))
                v.tensor_scalar(combine[:, t, :], combine[:, t, :], top_stat[:, t, 2:3], None, ALU.mult
                                ).then_inc(comb_ready, 1)
            v.wait_ge(comb_ready, TT)
            for r in range(ROUNDS):
                v.tensor_copy(weight_of[:, :, r * NE:(r + 1) * NE], combine[:, :, :])
            v.wait_ge(places, 1)
            v.tensor_reduce(peak[0:1, 0:1], bank[3][0:1, 0:NE], AX.X, ALU.max)
            first = slot_of[:, :, 0:NE]
            link(v.scalar_tensor_tensor(first, bank[2][:, 0:TT * NE].rearrange("p (t e) -> p t e", t=TT), 2.0 * S,
                                        chosen[:, :, :], ALU.add, ALU.mult))
            link(v.tensor_scalar(first, first, 2.0 * S, None, ALU.subtract))
            for r in range(1, ROUNDS):
                last = v.tensor_scalar(slot_of[:, :, r * NE:(r + 1) * NE], first, float(r * SLOTS), None, ALU.subtract)
            last.then_inc(routed, 1)
            v.wait_ge(routed, 1)

            def one_hots(first):
                for t in range(TT):
                    for i in range(2):
                        v.tensor_scalar(pick[:, t, i * SLOTS:(i + 1) * SLOTS], slot_no[:, :],
                                        slot_of[:, t, bass.ds(first + i, 1)], None, ALU.is_equal)
                    for i, at in ((0, first), (1, first + 1), (2, first)):
                        last = v.tensor_scalar(put[:, t, i * SLOTS:(i + 1) * SLOTS], slot_no[:, :],
                                               slot_of[:, t, bass.ds(at, 1)], weight_of[:, t, bass.ds(at, 1)],
                                               ALU.is_equal, ALU.mult)
                last.then_inc(picks, 1)

            def take_xT(b, before):
                for i, part in enumerate((G, Y)):
                    v.tensor_tensor(xT_e[:, b, 4 * i:4 * i + 4], part[:, :].rearrange("p (k n) -> p k n", k=4),
                                    mul_f[:, 4 * i:4 * i + 4].unsqueeze(2).broadcast_to([P, 4, P]), ALU.mult
                                    ).then_inc(dve_e, 1)
                v.wait_ge(dve_e, before + 2)
                v.tensor_tensor(xT_e[:, b], xT_e[:, b], add_f.unsqueeze(2).broadcast_to([P, KT, P]), ALU.add
                                ).then_inc(xT_ready, 1)

            def mark_expert(b, e):
                v.tensor_copy(is_expert[:, b, :], ident[:, bass.ds(e, 1)].broadcast_to([P, SLOTS])
                              ).then_inc(is_ready, 1)

            def experts(it, p):
                for e in range(EPB):
                    u, odd = divmod(e, 2)
                    before = it * (2 * DVE_PAIR) + (2 + DVE_PAIR * u + 2 * odd)
                    mark_expert((e + 1) % 2, p * EPB + (e + 1))
                    if odd:
                        v.wait_ge(g_turned, it * 2 + (u + 1))
                        one_hots(it * EPB + (e + 1))
                    wait_experts(v, it, e, 2)
                    v.tensor_scalar(gate, G[:, :], LIMIT, None, ALU.min).then_inc(gate_cut, 1)
                    v.wait_ge(gate_cut, it * EPB + (e + 1))
                    v.wait_ge(sig_ready, it * EPB + (e + 1))
                    v.tensor_tensor(gate, gate, sig, ALU.mult).then_inc(dve_e, 1)
                    wait_experts(v, it, e, 4)
                    v.tensor_scalar(up, U[:, :], LIMIT, -LIMIT, ALU.min, ALU.max).then_inc(dve_e, 1)
                    v.wait_ge(dve_e, before + 2)
                    v.scalar_tensor_tensor(act, up, 1.0, gate, ALU.add, ALU.mult).then_inc(act_ready, 1)
                    if odd:
                        v.wait_ge(gathered, it * 2 + (u + 2))
                        take_xT((u + 1) % 2, before + 2)

            v.wait_ge(routed, 1)
            one_hots(0)
            mark_expert(0, 0)
            v.wait_ge(gathered, 1)
            take_xT(0, 0)
            all_rounds(v, experts)

            v.wait_ge(moe_done, 1)
            v.wait_ge(gfin_in, 16)
            for t in range(TT):
                for half in range(2):
                    x2, xg, gt = (a.rearrange("p (c h n) -> p h c n", c=2, h=2)[:, half]
                                  for a in (x_rows[:, t, :], xn_rows[:, t, :], gates[:, 1, :]))
                    link(v.tensor_tensor(xg, bank[2 * t + half][:, :].rearrange("p (c n) -> p c n", c=2), gt, ALU.mult))
                    add = v.tensor_tensor(x2, x2, xg, ALU.add)
                add.then_inc(x2_ready, 1)
            for t in range(TT):
                v.wait_ge(squares, 5 + t)
                v.tensor_scalar(stat[:, 10 + t:11 + t], stat[:, 8 + t:9 + t], 1.0 / D, EPS, ALU.mult, ALU.add
                                ).then_inc(means, 1)
                v.wait_ge(roots, 4 + t)
                link(v.reciprocal(stat[:, 14 + t:15 + t], stat[:, 12 + t:13 + t]))
                v.scalar_tensor_tensor(xn_rows[:, t, :], x_rows[:, t, :], stat[:, 14 + t:15 + t], gfin,
                                       ALU.mult, ALU.mult).then_inc(fin_ready, 1)

        @block.tensor
        def _(pe):
            pe.wait_ge(hot_in, 48)
            pe.matmul(bank[7][0:NH, 0:384], table_sb[:, :], hot_sb, start=True, stop=True).then_inc(line_ready, 1)
            pe.wait_ge(consts, 4)
            for t in range(TT):
                pe.wait_ge(xn_ready, t + 1)
                for half in range(2):
                    for j in range(4):
                        k = 4 * half + j
                        last = pe.transpose(bank[2 * t + half][:, j * P:(j + 1) * P], xn_rows[:, t, k * P:(k + 1) * P],
                                            ident[:, :])
                    last.then_inc(x_turned, 1)

            n = 0
            job = 0
            summed = 0

            def free_bank(job):
                if job >= 4:
                    before = job - 4
                    if before in (4, 5):
                        pe.wait_ge(proj_dve, before - 3)
                    else:
                        pe.wait_ge(proj_act, before + 1 if before < 4 else before - 1)

            def columns(n, blocks, job):
                for b0 in range(0, len(blocks), 2):
                    free_bank(job)
                    for j, w_of in enumerate(blocks[b0:b0 + 2]):
                        for k in range(KT):
                            last = pe.matmul(bank[job % 4][:, j * S:(j + 1) * S], w_of(k), hT[:, k, :],
                                             start=(k == 0), stop=(k == KT - 1))
                    last.then_inc(*job_signal(job))
                    job += 1
                return job

            def ada_total(i):
                pe.wait_ge(ada_rows, i + 1)
                if i in GATE_CHUNKS:
                    if i != GATE_CHUNKS[0]:
                        pe.wait_ge(ada_taken, GATE_CHUNKS.index(i))
                    pe.matmul(bank[5][:, :], ones[:, :], ada_acc[i % 2], start=True, stop=True).then_inc(chunk_used, 1)
                else:
                    at = 4 * (i if i < 4 else i - 2)
                    for m in range(HB):
                        last = pe.matmul(bank[4][:, at + m:at + m + 1], ada_acc[i % 2][:, m * P:(m + 1) * P],
                                         ones[:, 0:1], start=True, stop=True)
                    last.then_inc(chunk_used, 1)

            for i in range(4):
                ada_total(i)
            n = 4
            pe.wait_ge(hT_dve, 1)
            pe.wait_ge(hT_act, 1)
            for kind in HEAD_CHUNKS[n:PRE - 2]:
                slot = ring[:, n % RING]
                if kind in ADA:
                    ada_total(ADA.index(kind))
                    n += 1
                    continue
                wait_chunk(pe, n)
                if kind in (Q_M, K_M, Q_S):
                    job = columns(n, [lambda k, m=m: slot[:, k, m * P:(m + 1) * P] for m in range(HB)], job)
                elif kind == V_M:
                    for t in range(TT):
                        free_bank(job)
                        for k in range(KT):
                            last = pe.matmul(bank[job % 4][:, :], hT[:, k, t * P:(t + 1) * P], slot[:, k, :],
                                             start=(k == 0), stop=(k == KT - 1))
                        last.then_inc(*job_signal(job))
                        job += 1
                else:
                    job = columns(n, [lambda k: slot[:, k, 0:P]], job)
                    free_bank(job)
                    for t in range(TT):
                        for k in range(KT):
                            last = pe.matmul(bank[job % 4][:, t * P:(t + 1) * P], hT[:, k, t * P:(t + 1) * P],
                                             slot[:, k, P:2 * P], start=(k == 0), stop=(k == KT - 1))
                    last.then_inc(*job_signal(job))
                    job += 1
                n += 1

            def score(h):
                if h >= 2:
                    pe.wait_ge(lows, h - 1)
                rows = slice(DH * (h % 2), DH * (h % 2) + DH)
                kb = h // 2 if h < NHM else 4
                pe.matmul(bank[h % 2][:, 0:256], qT[rows, h // 2, P:2 * P], kT[rows, kb, :], start=True, stop=True)
                pe.matmul(bank[h % 2][:, 256:384], qT[rows, h // 2, 0:P], kT[rows, kb, 0:P], start=True, stop=True
                          ).then_inc(scores, 1)

            def turn_p(h):
                pe.wait_ge(probs_ready, h + 1)
                if h >= 2:
                    pe.wait_ge(pT_ready, h - 1)
                for to, frm in ((0, 256), (128, 0), (256, 128)):
                    last = pe.transpose(bank[2 + h % 2][:, to:to + P], prob[:, h % PB, frm:frm + P], ident[:, :])
                last.then_inc(p_turned, 1)

            def values(h):
                pe.wait_ge(pT_ready, h + 1)
                blk, half = divmod(h, 2)
                if half == 0 and blk >= 2:
                    pe.wait_ge(o_taken, blk - 1)
                o = bank[6 + blk % 2][DH * half:DH * half + DH, 0:S]
                v0 = h * DH if h < NHM else 512 + half * DH
                pe.matmul(o, v_rows[:, 0, v0:v0 + DH], probT[:, h % 2, 0:256], start=True, stop=False)
                pe.matmul(o[:, P:2 * P], v_rows[:, 1, v0:v0 + DH], probT[:, h % 2, 256:384], start=False, stop=True
                          ).then_inc(o_ready, 1)

            pe.wait_ge(proj_act, 7)
            pe.wait_ge(proj_dve, 3)
            for h in range(NH + 3):
                if h < NH:
                    score(h)
                if 2 <= h < NH + 2:
                    turn_p(h - 2)
                if h >= 3:
                    values(h - 3)

            pe.wait_ge(o_taken, NHM)
            for half in range(2):
                wait_chunk(pe, n)
                for t in range(TT):
                    for k in range(KT):
                        last = pe.matmul(bank[2 * t + half][:, :], hT[:, k, t * P:(t + 1) * P],
                                         ring[:, n % RING, k, :], start=(k == 0), stop=(k == KT - 1))
                    last.then_inc(mixed if t == 0 else chunk_used, 1)
                n += 1
            assert n == PRE
            for t in range(TT):
                pe.wait_ge(xn1_ready, t + 1)
                for half in range(2):
                    for j in range(4):
                        k = 4 * half + j
                        last = pe.transpose(bank[4 + 2 * t + half][:, j * P:(j + 1) * P],
                                            xn_rows[:, t, k * P:(k + 1) * P], ident[:, :])
                    last.then_inc(x1_turned, 1)
            for t in range(TT):
                pe.wait_ge(h2_dve, t + 1)
                pe.wait_ge(h2_act, t + 1)
                for k in range(KT):
                    last = pe.matmul(bank[t][:, 0:NE], hT[:, k, t * P:(t + 1) * P], wr_sb[:, k, :],
                                     start=(k == 0), stop=(k == KT - 1))
                last.then_inc(logits_ready, 1)
            pe.wait_ge(chosen_ready, TT)
            pe.matmul(bank[2][:, 0:NE], earlier[:, :], chosen[:, 0, :], start=True, stop=True)
            pe.matmul(bank[2][:, NE:2 * NE], ones[:, :], chosen[:, 0, :], start=True, stop=False)
            pe.matmul(bank[2][:, NE:2 * NE], earlier[:, :], chosen[:, 1, :], start=False, stop=True)
            pe.matmul(bank[3][:, 0:NE], ones[:, :], chosen[:, 0, :], start=True, stop=False)
            pe.matmul(bank[3][:, 0:NE], ones[:, :], chosen[:, 1, :], start=False, stop=True).then_inc(places, 1)
            pe.wait_ge(comb_ready, TT)
            for t in range(TT):
                last = pe.transpose(bank[4][0:NE, t * P:(t + 1) * P], combine[:, t, :], ident[:, :])
            last.then_inc(comb_turned, 1)

            total = [[bank[2 * t + half] for half in range(2)] for t in range(TT)]
            pe.wait_ge(combT_ready, 1)
            pe.wait_ge(bdown_in, 16)
            pe.wait_ge(routed, 1)

            def half_columns(rows, first, half):
                return rows[:, first:first + 2 * CW].rearrange("p (c h n) -> p h c n", c=2, h=2)[:, half]

            for t in range(TT):
                for half in range(2):
                    last = pe.matmul(total[t][half][:, :], combT[:, t * P:(t + 1) * P],
                                     half_columns(bdown_sb, 0, half), start=True, stop=False)
            last.then_inc(scattered, 1)

            def gather():
                for k in range(KT):
                    for t in range(TT):
                        last = pe.matmul((G, Y)[k // 4][:, (k % 4) * P:(k % 4 + 1) * P], xn_rows[:, t, k * P:(k + 1) * P],
                                         pick[:, t, :], start=(t == 0), stop=(t == TT - 1))
                last.then_inc(gathered, 1)

            def scatter(stop, signal):
                for t in range(TT):
                    for half in range(2):
                        last = pe.matmul(total[t][half][:, :], gT[:, t, half, :], y_rows[:, half, :],
                                         start=False, stop=stop)
                last.then_inc(signal, 1)

            def experts(it, p):
                for e in range(EPB):
                    u, odd = divmod(e, 2)
                    first = PRE + CPE * e
                    pe.wait_ge(is_ready, it * EPB + (e + 1))
                    if not odd:
                        pe.wait_ge(xT_ready, it * 2 + (u + 1))
                    for g, to in enumerate((G, U)):
                        for half in range(2):
                            pe.matmul(to[half * SLOTS:(half + 1) * SLOTS, :], is_expert[:, e % 2, :],
                                      half_columns(bgu, g * FF, half), start=True, stop=False)
                        for c in range(2):
                            n = first + 2 * g + c
                            wait_chunk(pe, n, it)
                            for k in range(KT):
                                for half in range(2):
                                    last = pe.matmul(to[half * SLOTS:(half + 1) * SLOTS, c * QW:(c + 1) * QW],
                                                     xT_e[:, u % 2, k, odd * SLOTS:(odd + 1) * SLOTS],
                                                     ring[:, n % RING, k, half * QW:(half + 1) * QW],
                                                     start=False, stop=(c == 1 and k == KT - 1))
                            last.then_inc(chunk_used, 1)
                    pe.wait_ge(y_ready, it * EPB + (e + 1))
                    if not odd:
                        pe.wait_ge(gT_ready, it * 2 + (u + 1))
                        scatter(False, scattered)
                        pe.wait_ge(gate_cut, it * EPB + (e + 1))
                        for t in range(TT):
                            for s in range(2):
                                last = pe.transpose(G[:, (2 * t + s) * P:(2 * t + s + 1) * P],
                                                    put[:, t, s * SLOTS:s * SLOTS + P], ident[:, :])
                        last.then_inc(g_turned, 1)
                    else:
                        pe.wait_ge(gate_cut, it * EPB + (e + 1))
                        pe.wait_ge(gT_ready, it * 2 + (u + 2))
                        pe.wait_ge(picks, it * 2 + (u + 2))
                        gather()
                    pe.wait_ge(act_ready, it * EPB + (e + 1))
                    for j in range(4):
                        last = pe.transpose(T[:, j * P:(j + 1) * P], act[:, j * P:(j + 1) * P], ident[:, :])
                    last.then_inc(act_turned, 1)
                    pe.wait_ge(actT_ready, it * EPB + (e + 1))
                    if odd:
                        pe.wait_ge(xT_ready, it * 2 + (u + 2))
                    for c in range(2):
                        n = first + 4 + c
                        wait_chunk(pe, n, it)
                        for k in range(KT):
                            blk, part = 2 * (k // 4) + k % 2, k % 4 // 2
                            for half in range(2):
                                rows = half ^ odd
                                last = pe.matmul(Y[rows * SLOTS:(rows + 1) * SLOTS, c * QW:(c + 1) * QW],
                                                 actT[:, blk * P + part * SLOTS:blk * P + (part + 1) * SLOTS],
                                                 ring[:, n % RING, k, half * QW:(half + 1) * QW],
                                                 start=(k == 0), stop=(k == KT - 1))
                        last.then_inc(chunk_used, 1)

            pe.wait_ge(picks, 1)
            gather()
            pe.wait_ge(bgu_in, 16)
            bodies = all_rounds(pe, experts)
            pe.wait_ge(y_ready, bodies * EPB + 1)
            pe.wait_ge(gT_ready, bodies * 2 + 1)
            scatter(True, moe_done)


def kernel(x, c, g_attn, w_ada, b_ada, w_in, b_in, w_out, b_out, rel_table, sinks, g_ffn, w_router, b_router,
           w_gate_up, b_gate_up, w_down, b_down, g_final):
    import concourse.bacc as bacc
    from concourse.bass_utils import run_bass_kernel_spmd

    def columns(a, tiles):
        return np.ascontiguousarray(np.asarray(a).reshape(tiles, P).T)

    b_in_0 = np.asarray(b_in)[0]
    swa_q = b_in_0[1536:2048].reshape(2, 4, DH).transpose(1, 0, 2).reshape(-1)
    b_in_blocks = np.concatenate([b_in_0[:1536], swa_q, b_in_0[2048:]])
    w_q = np.asarray(w_in)[0]
    w_q = np.concatenate([w_q[:, :1536], w_q[:, 1536:2048].reshape(D, 2, 4, DH).transpose(0, 2, 1, 3).reshape(D, 512),
                          w_q[:, 2048:]], axis=1)
    w_o = np.asarray(w_out)[0]
    w_o = np.concatenate([w_o[:512], w_o[512:].reshape(2, 4, DH, D).transpose(1, 0, 2, 3).reshape(512, D)])

    arrays = {
        "x": np.asarray(x)[0],
        "vectors": np.concatenate([columns(c, KT), columns(g_attn, KT), columns(g_ffn, KT), columns(b_ada, 6 * KT),
                                   columns(b_in_blocks, D_IN // P)], axis=1),
        "w_ada": np.asarray(w_ada)[0], "b_ada_row": np.asarray(b_ada)[0],
        "w_in": w_q, "b_in_row": b_in_0,
        "w_out": w_o, "b_out": np.asarray(b_out)[0], "rel_table": np.asarray(rel_table), "sinks": np.asarray(sinks)[0],
        "w_router": np.asarray(w_router)[0], "b_router": np.asarray(b_router)[0],
        "w_gate_up": np.asarray(w_gate_up)[0],
        "b_gate_up": np.asarray(b_gate_up)[0],
        "w_down": np.asarray(w_down)[0], "b_down": np.asarray(b_down)[0], "g_final": np.asarray(g_final),
        "bucket_hot": bucket_table(), "masks": mask_rows(),
    }
    arrays = {name: np.ascontiguousarray(a) for name, a in arrays.items()}
    nc = bacc.Bacc("TRN2", target_bir_lowering=False, num_devices=1)
    args = {name: nc.dram_tensor(name, a.shape, mybir.dt.from_np(a.dtype), kind="ExternalInput").ap()
            for name, a in arrays.items()}
    toeplitz = nc.dram_tensor("bias_lines", [NH, 384], F32, kind="Internal").ap()
    out = nc.dram_tensor("out", [S, D], F32, kind="ExternalOutput").ap()
    build(nc, **args, toeplitz=toeplitz, out=out)
    result = run_bass_kernel_spmd(nc, [arrays], core_ids=[0])
    return result.results[0]["out"].reshape(1, S, D)
```

```python
from contextlib import ExitStack
import math

import concourse.bass as bass
from concourse import mybir
import numpy as np

P = 128
D = 1024
S = 256
TT = S // P
KT = D // P
DH = 64
NH = 16
NHM = 8
D_IN = 2304
NE = 32
TOPK = 4
FF = 1024
LIMIT = 7.0
ALPHA = 1.702
EPS = 1e-5
NEG = -1e30
BIG = 3.0e38
BUCKETS = 32
MAX_DIST = 1024
WINDOW = 128

SLOTS = 64
PB = 4
ROUNDS = S // SLOTS
RING = 8
HT = KT // 2
CW = 512
EPB = 4
CPE = 6
ITERS = NE // EPB
HB = 4
QW = CW // 2

F32 = mybir.dt.float32
I32 = mybir.dt.int32
ALU = mybir.AluOpType
ACT = mybir.ActivationFunctionType
AX = mybir.AxisListType

SHIFT_A, SCALE_A, GATE_A, SHIFT_F, SCALE_F, GATE_F = range(6)
ADA = [("ada", part * D + half * CW) for part in (SCALE_A, SHIFT_A, GATE_A, SHIFT_F, SCALE_F, GATE_F) for half in (0, 1)]
GATE_CHUNKS = [i for i, (_, first) in enumerate(ADA) if first // D in (GATE_A, GATE_F)]
Q_M, K_M, V_M, Q_S, KV_S = [("in", CW * i) for i in range(5)]
HEAD_CHUNKS = ADA[0:4] + [Q_M, K_M, ADA[4], V_M, ADA[5], Q_S, ADA[6], KV_S, ADA[7],
                          ("out", 0), ADA[8], ("out", CW), ADA[9], ADA[10], ADA[11]]
POOL_ADA = 7, 8, 9, 11
PRE = len(HEAD_CHUNKS)


def bucket_table():
    hot = np.zeros((BUCKETS + 2, 384), np.float32)
    exact = BUCKETS // 2
    for m in range(384):
        d = 255 - m
        if d >= 0:
            if d < exact:
                b = d
            else:
                nf = np.float32(d) / np.float32(exact)
                b = exact + int(np.float32(np.log(nf)) / np.float32(math.log(MAX_DIST / exact)) * np.float32(BUCKETS - exact))
                b = min(b, BUCKETS - 1)
            hot[b, m] = 1.0
        hot[BUCKETS, m] = d < 0
        hot[BUCKETS + 1, m] = d < 0 or d >= WINDOW
    return hot


def mask_rows():
    rows = np.zeros((2, NH), np.float32)
    rows[0, :NHM] = NEG
    rows[1, NHM:] = NEG
    return rows


def build(nc, x, vectors, w_ada, b_ada_row, w_in, b_in_row, w_out, b_out, rel_table,
          sinks, w_router, b_router, w_gate_up, b_gate_up, w_down, b_down, g_final, bucket_hot, masks,
          toeplitz, out):
    with ExitStack() as ctx:
        def sb(name, shape, dt=F32):
            return ctx.enter_context(nc.sbuf_tensor(name, shape, dt))

        def sem(name):
            return ctx.enter_context(nc.semaphore(name))

        bank = [ctx.enter_context(nc.psum_tensor(f"bank{i}", [P, 512], F32)) for i in range(8)]

        ring = sb("ring", [P, RING, KT, CW])
        x_rows = sb("x_rows", [P, TT, D])
        xn_rows = sb("xn_rows", [P, TT, D])
        hT = sb("hT", [P, KT, S])
        gates = sb("gates", [P, 2, D])
        ident = sb("ident", [P, P])
        ones = sb("ones", [P, P])
        earlier = sb("earlier", [P, P])
        slot_no = sb("slot_no", [P, SLOTS])
        col = sb("col", [P, 160])
        VECS = 90
        c_sb, ga_sb, gf_sb = col[:, 0:8], col[:, 8:16], col[:, 16:24]
        ba_sb, bi_sb = col[:, 24:72], col[:, 72:90]
        sc_sb = col[:, 90:98]
        nbq_sb = col[:, 98:106]
        mul_a, add_a = col[:, 106:114], col[:, 114:122]
        mul_f, add_f = col[:, 122:130], col[:, 130:138]
        stat = sb("stat", [P, 16])
        eps = stat[:, 14:15]
        sink_sb = sb("sink_sb", [P, NHM])
        nsink_sb = sb("nsink_sb", [P, NHM])
        table_sb = sb("table_sb", [BUCKETS + 2, NH])
        wr_sb = sb("wr_sb", [P, KT, NE])
        br_sb = sb("br_sb", [P, NE])
        lowest = sb("lowest", [P, NH, TT])
        rowsum = sb("rowsum", [P, NH, TT])
        sinkexp = sb("sinkexp", [P, NHM, TT])
        peak = sb("peak", [1, 2], I32)
        prob = sb("prob", [P, PB, 384])
        probT = sb("probT", [P, 2, 384])
        prob_flat = prob[:, :, :].rearrange("p a n -> p (a n)")
        ada_acc = prob_flat[:, 0:CW], prob_flat[:, CW:2 * CW]
        hot_sb = probT[0:BUCKETS + 2, 0, :]
        line_sb = probT[0:NH, 1, :]
        late = sb("late", [P, 8704])
        bias = late[:, 0:4096].rearrange("p (h n) -> p h n", h=NH)
        qT = late[:, 4096:6144].rearrange("p (b n) -> p b n", b=8)
        kT = late[:, 6144:7424].rearrange("p (b n) -> p b n", b=5)
        v_rows = late[:, 7424:8704].rearrange("p (t n) -> p t n", t=TT)

        used = [0]

        def piece(n):
            used[0] += n
            return late[:, used[0] - n:used[0]]

        xT_e = piece(2 * KT * 2 * SLOTS).rearrange("p (b k n) -> p b k n", b=2, k=KT)
        gate, sig, up, act = piece(512), piece(512), piece(512), piece(512)
        actT = piece(512)
        y_rows = piece(2 * 512).rearrange("p (h n) -> p h n", h=2)
        gT = piece(TT * 2 * P).rearrange("p (t s n) -> p t s n", t=TT, s=2)
        is_expert = piece(2 * SLOTS).rearrange("p (b n) -> p b n", b=2)
        slot_of = piece(TT * (ROUNDS * NE + 2)).rearrange("p (t n) -> p t n", t=TT)
        weight_of = piece(TT * (ROUNDS * NE + 2)).rearrange("p (t n) -> p t n", t=TT)
        pick = piece(TT * 2 * SLOTS).rearrange("p (t n) -> p t n", t=TT)
        put = piece(TT * 3 * SLOTS).rearrange("p (t n) -> p t n", t=TT)
        route = piece(TT * 160).rearrange("p (t n) -> p t n", t=TT)
        combT = piece(S)[0:NE, :]
        assert used[0] <= 8704
        logit, left = route[:, :, 0:40], route[:, :, 40:76]
        top8, chosen, combine = route[:, :, 76:84], route[:, :, 84:116], route[:, :, 116:148]
        top_stat = route[:, :, 148:152]
        bdown_sb = gates[0:NE, 0, :]
        gfin = prob_flat[:, CW:CW + D]
        bgu = hT[:, :, :].rearrange("p k n -> p (k n)")

        half_in = [[sem(f"half_in{i}_{hf}") for hf in range(2)] for i in range(RING)]
        half_used = sem("half_used")
        x_in, vec_in, same_in, hot_in = sem("x_in"), sem("vec_in"), sem("same_in"), sem("hot_in")
        line_out, bias_in, b_out_in = sem("line_out"), sem("bias_in"), sem("b_out_in")
        moe_gated, x2_half_ready = sem("moe_gated"), sem("x2_half_ready")
        b_out_gated, b_out_added, pads = sem("b_out_gated"), sem("b_out_added"), sem("pads")
        gfin_in, result_out, wr_in = sem("gfin_in"), sem("result_out"), sem("wr_in")
        consts, line_ready, line_copied = sem("consts"), sem("line_ready"), sem("line_copied")
        dve = sem("dve")
        counts, y_low_ready = sem("counts"), sem("y_low_ready")
        mod_f_ready, shift_taken = sem("mod_f_ready"), sem("shift_taken")
        pool_sum, pool_rows = sem("pool_sum"), sem("pool_rows")
        squares, first_half, roots = sem("squares"), sem("first_half"), sem("roots")
        sc_sig, sc_ready = sem("sc_sig"), sem("sc_ready")
        xn_ready, x_turned, hT_dve, hT_act = sem("xn_ready"), sem("x_turned"), sem("hT_dve"), sem("hT_act")
        mod_ready, ada_rows, ada_taken = sem("mod_ready"), sem("ada_rows"), sem("ada_taken")
        proj, proj_act, proj_dve = sem("proj"), sem("proj_act"), sem("proj_dve")
        scores, lows, exps, probs_ready = sem("scores"), sem("lows"), sem("exps"), sem("probs_ready")
        p_turned, pT_ready, o_ready, o_taken = sem("p_turned"), sem("pT_ready"), sem("o_ready"), sem("o_taken")
        mixed, x1_ready, xn1_ready, x1_turned = sem("mixed"), sem("x1_ready"), sem("xn1_ready"), sem("x1_turned")
        h2_dve, h2_act, logits_ready, top_ready = sem("h2_dve"), sem("h2_act"), sem("logits_ready"), sem("top_ready")
        top_exp, chosen_ready, places = sem("top_exp"), sem("chosen_ready"), sem("places")
        comb_ready, comb_turned, combT_ready = sem("comb_ready"), sem("comb_turned"), sem("combT_ready")
        routed = sem("routed")
        bdown_in, bgu_in = sem("bdown_in"), sem("bgu_in")
        picks, gathered, xT_ready = sem("picks"), sem("gathered"), sem("xT_ready")
        gate_cut, is_ready = sem("gate_cut"), sem("is_ready")
        sig_ready, act_ready = sem("sig_ready"), sem("act_ready")
        dve_e = sem("dve_e")
        act_turned, actT_ready, y_ready = sem("act_turned"), sem("actT_ready"), sem("y_ready")
        g_turned, gT_ready, scattered = sem("g_turned"), sem("gT_ready"), sem("scattered")
        moe_done, x2_ready, fin_ready = sem("moe_done"), sem("x2_ready"), sem("fin_ready")

        block = ctx.enter_context(nc.Block())
        G, U, T, Y = bank[4], bank[5], bank[6], bank[7]

        def wait_half(eng, n, hf, it=None):
            landed = 16 * (n // RING + 1)
            eng.wait_ge(half_in[n % RING][hf], landed if it is None else it * (16 * EPB * CPE // RING) + landed)

        def wait_chunk(eng, n):
            for hf in range(2):
                wait_half(eng, n, hf)

        def chunk_no(kind):
            return HEAD_CHUNKS.index(kind)

        JOB_CHUNK = [chunk_no(kind) for kind in (Q_M, K_M, V_M, Q_S, KV_S)]

        KV_STEPS = {1: 0, 2: 1, 3: 2, 4: 3}
        OUT_STEPS = {8: ((0, 0),), 9: ((1, 0),), 10: ((0, 1),), 11: ((1, 1), (2, 0)), 12: ((2, 1),),
                     13: ((3, 0), (3, 1)), 15: ((4, 0), (4, 1)), 17: ((5, 0), (5, 1))}
        job_bank = [bank[i] for i in (5, 6, 7, 3, 0, 1, 2, 3, 5, 4)]
        mixer_bank = (bank[5], bank[4]), (bank[0], bank[1])
        gate_bank = {4: bank[5], 5: bank[5], 10: bank[3], 11: bank[4]}
        turned = (bank[4], bank[6]), (bank[7], bank[5])
        X1_ORDER = ((0, 0), (0, 1), (1, 0), (1, 1))
        X2_ORDER = ((0, 0), (1, 0), (0, 1), (1, 1))

        def job_signal(job):
            return (half_used, 2) if job % 2 else (proj, 1)

        def wait_job(eng, job):
            if job % 2:
                eng.wait_ge(half_used, 2 * (JOB_CHUNK[job // 2] + 1))
            else:
                eng.wait_ge(proj, job // 2 + 1)

        def wait_experts(eng, it, e, chunks):
            eng.wait_ge(half_used, it * (2 * EPB * CPE) + 2 * (PRE + CPE * e + chunks))

        def all_rounds(eng, body, begin=0):
            with eng.Fori(begin, ITERS) as p:
                body(p, p)
            eng.wait_ge(routed, 1)
            busiest = eng.value_load(peak[0:1, 0:1], min_val=1, max_val=S)
            with eng.If(busiest > SLOTS):
                with eng.Fori(1, (busiest + (SLOTS - 1)) // SLOTS) as r:
                    with eng.Fori(0, ITERS) as p:
                        body(r * ITERS + p, p)
            return (busiest + (SLOTS - 1)) // SLOTS * ITERS

        def head_of(h):
            return h if h < NHM else NHM + (h - NHM) // 2 + 4 * (h % 2)

        @block.sync
        def _(sp):
            for t in range(TT):
                sp.dma_start(x_rows[:, t, :], x[t * P:(t + 1) * P, :]).then_inc(x_in, 16)
            sp.dma_start(col[:, 0:VECS], vectors).then_inc(vec_in, 16)
            source = {"ada": w_ada, "in": w_in, "out": w_out}
            for n, (kind, first) in enumerate(HEAD_CHUNKS):
                if n == 3:
                    sp.wait_ge(line_copied, 1)
                if (kind, first) == KV_S:
                    sp.wait_ge(line_out, 16)
                    sp.dma_start(bias[:, :, :], bass.AP(toeplitz.tensor, toeplitz.offset, [[1, P], [384, NH], [1, S]])
                                 ).then_inc(bias_in, 16)
                w = min(CW, source[kind].shape[1] - first)
                for hf in range(2):
                    if n >= RING:
                        sp.wait_ge(half_used, 2 * (n - RING) + hf + 1)
                    sp.dma_start(ring[:, n % RING, hf * HT:(hf + 1) * HT, 0:w],
                                 source[kind][hf * HT * P:(hf + 1) * HT * P, first:first + w].rearrange(
                                     "(k p) n -> p k n", p=P)).then_inc(half_in[n % RING][hf], 16)

                if n == RING - 1:
                    for t in range(TT):
                        sp.dma_start(v_rows[:, t, 0:512], b_in_row[1024:1536].partition_broadcast(P)
                                     ).then_inc(same_in, 16)
                        sp.dma_start(v_rows[:, t, 512:640], b_in_row[2176:2304].partition_broadcast(P)
                                     ).then_inc(same_in, 16)
                    for i, part in enumerate((GATE_A, GATE_F)):
                        sp.dma_start(gates[:, i, :], b_ada_row[part * D:(part + 1) * D].partition_broadcast(P)
                                     ).then_inc(same_in, 16)
                    for dst, src in ((sink_sb[:, :], sinks.partition_broadcast(P)),
                                     (br_sb[:, :], b_router.partition_broadcast(P)),
                                     (wr_sb[:, :, :], w_router.rearrange("(k p) n -> p k n", p=P))):
                        sp.dma_start(dst, src).then_inc(wr_in, 16)

            def load_experts(it, p):
                for e in range(EPB):
                    for j in range(CPE):
                        n = PRE + CPE * e + j
                        for hf in range(2):
                            sp.wait_ge(half_used, it * (2 * EPB * CPE) + (2 * (n - RING) + hf + 1))
                            rows = slice(hf * HT * P, (hf + 1) * HT * P)
                            if j < 4:
                                src = w_gate_up[bass.ds(p * EPB + e, 1), rows, j * CW:(j + 1) * CW]
                            else:
                                src = w_down[bass.ds(p * EPB + e, 1), rows, (j - 4) * CW:(j - 3) * CW]
                            sp.dma_start(ring[:, n % RING, hf * HT:(hf + 1) * HT],
                                         src.rearrange("a (k p) n -> p (a k) n", p=P)
                                         ).then_inc(half_in[n % RING][hf], 16)

            all_rounds(sp, load_experts)
            for t in range(TT):
                sp.wait_ge(fin_ready, t + 1)
                sp.dma_start(out[t * P:(t + 1) * P, :], xn_rows[:, t, :]).then_inc(result_out, 16)
            sp.wait_ge(result_out, 16 * TT)

        @block.gpsimd
        def _(pool):
            pool_steps = [0]

            def pool_ada_chunk(i):
                n = chunk_no(ADA[i])
                wait_chunk(pool, n)
                w = ring[:, n % RING]
                pool.tensor_tensor(w, w, sc_sb.unsqueeze(2).broadcast_to([P, KT, CW]), ALU.mult).then_inc(pool_sum, 1)
                for rows in (4, 2, 1):
                    pool_steps[0] += 1
                    pool.wait_ge(pool_sum, pool_steps[0])
                    pool.tensor_tensor(w[:, 0:rows], w[:, 0:rows], w[:, rows:2 * rows], ALU.add
                                       ).then_inc(pool_sum if rows > 1 else pool_rows, 1)

            pool.memset(eps, EPS).then_inc(consts, 1)
            pool.memset(ones[:, :], 1.0).then_inc(consts, 1)
            pool.wait_ge(consts, 2)
            pool.affine_select(out=ident[:, :], in_=ones[:, :], compare_op=ALU.is_equal, fill=0.0,
                               base=0, pattern=[[-1, P]], channel_multiplier=1).then_inc(consts, 1)
            pool.affine_select(out=earlier[:, :], in_=ones[:, :], compare_op=ALU.is_gt, fill=0.0,
                               base=0, pattern=[[1, P]], channel_multiplier=-1).then_inc(consts, 1)
            pool.iota(slot_no[:, :], pattern=[[1, SLOTS]], base=2 * S, channel_multiplier=0,
                      allow_small_or_imprecise_dtypes=True).then_inc(consts, 1)
            pool.wait_ge(x_turned, 4)
            pool.dma_start(xn_rows[:, 0, :], b_out.partition_broadcast(P)).then_inc(b_out_in, 16)
            pool.wait_ge(b_out_in, 16)
            pool.wait_ge(ada_taken, 2)
            pool.tensor_tensor(xn_rows[:, 0, :], xn_rows[:, 0, :], gates[:, 0, :], ALU.mult).then_inc(b_out_gated, 1)
            pool.wait_ge(b_out_gated, 1)
            for t in range(TT):
                pool.tensor_tensor(x_rows[:, t, :], x_rows[:, t, :], xn_rows[:, 0, :], ALU.add
                                   ).then_inc(b_out_added, 1)
            pool.wait_ge(sc_ready, 1)
            for i in POOL_ADA[:-1]:
                pool_ada_chunk(i)
            pool.wait_ge(scores, NH)
            pool.memset(slot_of[:, :, ROUNDS * NE:], -1.0).then_inc(pads, 1)
            pool.memset(weight_of[:, :, ROUNDS * NE:], 0.0).then_inc(pads, 1)
            pool.wait_ge(o_ready, NH)
            pool.memset(logit[:, :, NE:NE + 4], BIG).then_inc(pads, 1)
            pool_ada_chunk(POOL_ADA[-1])
            for t in range(TT):
                x2, xg = (a.rearrange("p (c h n) -> p h c n", c=2, h=2)[:, 0]
                          for a in (x_rows[:, t, :], xn_rows[:, t, :]))
                pool.wait_ge(moe_gated, t + 1)
                pool.tensor_tensor(x2, x2, xg, ALU.add).then_inc(x2_half_ready, 1)

        @block.scalar
        def _(a):
            a.dma_start(table_sb[0:BUCKETS, :], rel_table).then_inc(hot_in, 16)
            a.dma_start(table_sb[BUCKETS:BUCKETS + 2, :], masks).then_inc(hot_in, 16)
            a.dma_start(hot_sb, bucket_hot).then_inc(hot_in, 16)
            a.wait_ge(vec_in, 16)
            a.activation(sc_sb, c_sb, ACT.Sigmoid).then_inc(sc_sig, 1)
            a.wait_ge(x_in, 16 * TT)
            for t in range(TT):
                a.activation(xn_rows[:, t, :], x_rows[:, t, :], ACT.Square,
                             accum_out=stat[:, t:t + 1]).then_inc(squares, 1)
            a.wait_ge(consts, 1)
            a.wait_ge(squares, TT)
            a.activation(stat[:, 2:4], stat[:, 0:2], ACT.Sqrt, bias=eps, scale=1.0 / D).then_inc(roots, 1)
            a.wait_ge(line_ready, 1)
            a.activation(line_sb, bank[7][0:NH, 0:384], ACT.Copy, scale=-1.0).then_inc(line_copied, 1)
            a.wait_ge(line_copied, 1)
            a.dma_start(toeplitz, line_sb).then_inc(line_out, 16)
            a.wait_ge(mod_ready, 1)
            for k in range(KT):
                if k % 4 == 0:
                    a.wait_ge(x_turned, 3 + k // 4)
                a.activation(hT[:, k, P:2 * P], bank[2 + k // 4][:, (k % 4) * P:(k % 4 + 1) * P],
                             ACT.Identity, bias=add_a[:, k:k + 1], scale=mul_a[:, k:k + 1]).then_inc(hT_act, 1)

            def take_job(job, dst, blk, bias_col, n):
                wait_job(a, job)
                for j in range(n):
                    b_sb = (nbq_sb if dst is qT else bi_sb)[:, bias_col + j:bias_col + j + 1]
                    to, frm = (ap.rearrange("p (t n) -> p t n", t=TT)
                               for ap in (dst[:, blk + j, :], job_bank[job][:, j * S:(j + 1) * S]))
                    if dst is qT:
                        frm = frm[:, :, ::-1]
                    last = a.activation(to, frm, ACT.Identity,
                                        bias=b_sb, scale=-DH ** -0.5 if dst is qT else 1.0)
                last.then_inc(proj_act, 1)

            for job, dst, blk, bias_col, n in ((0, qT, 0, 0, 2), (1, qT, 2, 2, 2), (2, kT, 0, 4, 2), (3, kT, 2, 6, 2),
                                               (6, qT, 4, 4, 2), (7, qT, 6, 6, 2)):
                take_job(job, dst, blk, bias_col, n)

            def exp_head(h):
                a.wait_ge(lows, h + 1)
                a.activation(prob[:, h % PB, 0:256], prob[:, h % PB, 0:256], ACT.Exp, bias=lowest[:, h, 1:2],
                             scale=-1.0, accum_out=rowsum[:, h, 1:2])
                if h >= NHM:
                    sink = head_of(h) - NHM
                    a.activation(sinkexp[:, h - NHM, :], lowest[:, h, :], ACT.Exp, bias=sink_sb[:, sink:sink + 1])
                a.activation(prob[:, h % PB, 256:384], prob[:, h % PB, 256:384], ACT.Exp, bias=lowest[:, h, 0:1],
                             scale=-1.0, accum_out=rowsum[:, h, 0:1]).then_inc(exps, 1)

            def take_pT(h):
                a.wait_ge(p_turned, h + 1)
                if h >= 2:
                    a.wait_ge(o_ready, h - 1)
                a.activation(probT[:, h % 2, :], bank[2 + h % 2][:, 0:384], ACT.Copy).then_inc(pT_ready, 1)

            a.wait_ge(wr_in, 16 * 3)
            a.activation(stat[:, 15:16], eps, ACT.Exp)
            for h in range(NH + 2):
                if h < NH:
                    exp_head(h)
                if h == 3:
                    take_job(8, kT, 4, 16, 1)
                if h >= 2:
                    take_pT(h - 2)

            a.dma_start(gfin, g_final.partition_broadcast(P)).then_inc(gfin_in, 16)

            def rms_rows(ready, order, pieces, before):
                a.activation(stat[:, 15:16], eps, ACT.Sqrt)
                for n, (half, t) in enumerate(order):
                    xg, x2 = (r[:, t, :].rearrange("p (c h n) -> p h c n", c=pieces, h=2)[:, half]
                              for r in (xn_rows, x_rows))
                    a.wait_ge(*ready(n, half, t))
                    a.activation(xg, x2, ACT.Square,
                                 accum_out=stat[:, 4 + 2 * t + half:5 + 2 * t + half]).then_inc(squares, 1)
                    a.wait_ge(squares, 2 * before - TT + n + 1)
                    if half == 0:
                        a.activation(stat[:, 8 + t:9 + t], stat[:, 4 + 2 * t:5 + 2 * t], ACT.Identity, bias=eps,
                                     scale=1.0 / D).then_inc(first_half, 1)
                    else:
                        a.wait_ge(first_half, before + t - TT + 1)
                        a.activation(stat[:, 10 + t:11 + t], stat[:, 5 + 2 * t:6 + 2 * t], ACT.Sqrt,
                                     bias=stat[:, 8 + t:9 + t], scale=1.0 / D).then_inc(roots, 1)

            rms_rows(lambda n, half, t: (x1_ready, n + 1), X1_ORDER, 1, TT)
            a.dma_start(bdown_sb, b_down).then_inc(bdown_in, 16)
            for t in range(TT):
                a.wait_ge(x1_turned, 2 * t + 2)
                a.wait_ge(mod_f_ready, 1)
                for k in range(4, KT):
                    last = a.activation(hT[:, k, t * P:(t + 1) * P], turned[t][1][:, (k % 4) * P:(k % 4 + 1) * P],
                                        ACT.Identity, bias=add_f[:, k:k + 1], scale=mul_f[:, k:k + 1])
                last.then_inc(h2_act, 1)
            for t in range(TT):
                a.wait_ge(top_ready, t + 1)
                a.activation(combine[:, t, :], logit[:, t, 0:NE], ACT.Exp, bias=top_stat[:, t, 0:1]
                             ).then_inc(top_exp, 1)
            a.dma_start(bgu[0:NE, :], b_gate_up).then_inc(bgu_in, 16)
            a.wait_ge(comb_turned, 1)
            a.activation(combT, U[0:NE, 0:S], ACT.Copy).then_inc(combT_ready, 1)

            def experts(it, p):
                for e in range(EPB):
                    u, odd = divmod(e, 2)
                    a.wait_ge(gate_cut, it * EPB + (e + 1))
                    a.activation(sig, gate, ACT.Sigmoid, scale=ALPHA).then_inc(sig_ready, 1)
                    if not odd:
                        a.wait_ge(g_turned, it * 2 + (u + 1))
                        a.wait_ge(scattered, it * 2 + (u + 1))
                        a.activation(gT.rearrange("p t s n -> p (t s n)"), G[:, :], ACT.Copy).then_inc(gT_ready, 1)
                    a.wait_ge(act_turned, it * EPB + (e + 1))
                    a.activation(actT, T[:, :], ACT.Copy).then_inc(actT_ready, 1)
                    wait_experts(a, it, e, 6)
                    if not odd:
                        a.wait_ge(scattered, it * 2 + (u + 1))
                    a.activation(y_rows[SLOTS:P, 1 - odd, :], Y[SLOTS:P, :], ACT.Copy).then_inc(y_ready, 1)

            all_rounds(a, experts)
            rms_rows(lambda n, half, t: (x2_ready if half else x2_half_ready, t + 1), X2_ORDER, 2, 2 * TT)

        @block.vector
        def _(v):
            own = [0]

            def link(ins):
                own[0] += 1
                ins.then_inc(dve, 1)
                v.wait_ge(dve, own[0])

            v.wait_ge(sc_sig, 1)
            v.tensor_tensor(sc_sb, c_sb, sc_sb, ALU.mult).then_inc(sc_ready, 1)
            v.tensor_scalar(nbq_sb[:, 0:4], bi_sb[:, 0:4], -DH ** -0.5, None, ALU.mult)
            v.tensor_scalar(nbq_sb[:, 4:8], bi_sb[:, 12:16], -DH ** -0.5, None, ALU.mult)

            def ada_chunk(i):
                rows = KT - 1 if i < 4 else KT
                n = chunk_no(ADA[i])
                wait_half(v, n, 0)
                acc, w = ada_acc[i % 2], ring[:, n % RING]
                if i > 6:
                    v.wait_ge(p_turned, NH)
                elif i >= 2:
                    v.wait_ge(half_used, 2 * (chunk_no(ADA[i - 2]) + 1))
                link(v.tensor_scalar(acc, w[:, 0, :], sc_sb[:, 0:1], None, ALU.mult))
                for k in range(1, rows - 1):
                    if k == HT:
                        wait_half(v, n, 1)
                    link(v.scalar_tensor_tensor(acc, w[:, k, :], sc_sb[:, k:k + 1], acc, ALU.mult, ALU.add))
                v.scalar_tensor_tensor(acc, w[:, rows - 1, :], sc_sb[:, rows - 1:rows], acc, ALU.mult, ALU.add
                                       ).then_inc(ada_rows, 1)

            v.wait_ge(sc_ready, 1)
            ada_chunk(0)
            v.wait_ge(roots, 1)
            link(v.reciprocal(stat[:, 6:8], stat[:, 2:4]))
            for t in range(TT):
                v.tensor_scalar(xn_rows[:, t, :], x_rows[:, t, :], stat[:, 6 + t:7 + t], None, ALU.mult
                                ).then_inc(xn_ready, 1)
            for i in range(1, 4):
                ada_chunk(i)
            v.wait_ge(half_used, 8)
            link(v.tensor_tensor(mul_a, bank[4][:, 0:8], ba_sb[:, SCALE_A * KT:(SCALE_A + 1) * KT], ALU.add))
            v.tensor_tensor(add_a, bank[4][:, 8:16], ba_sb[:, SHIFT_A * KT:(SHIFT_A + 1) * KT], ALU.add)
            v.scalar_tensor_tensor(mul_a, mul_a, 1.0, ga_sb, ALU.add, ALU.mult).then_inc(mod_ready, 1)
            v.wait_ge(mod_ready, 1)
            for k in range(KT):
                if k % 4 == 0:
                    v.wait_ge(x_turned, 1 + k // 4)
                v.tensor_scalar(hT[:, k, 0:P], bank[k // 4][:, (k % 4) * P:(k % 4 + 1) * P],
                                mul_a[:, k:k + 1], add_a[:, k:k + 1], ALU.mult, ALU.add).then_inc(hT_dve, 1)

            def take_gate(i):
                v.wait_ge(half_used, 2 * (chunk_no(ADA[i]) + 1))
                g = gates[:, i // 10, (i % 2) * CW:(i % 2 + 1) * CW]
                v.tensor_tensor(g, gate_bank[i][:, :], g, ALU.add).then_inc(ada_taken, 1)

            def take_v(job):
                wait_job(v, job)
                if job == 9:
                    for t in range(TT):
                        last = v.tensor_tensor(v_rows[:, t, 512:640], job_bank[job][:, t * P:(t + 1) * P],
                                               v_rows[:, t, 512:640], ALU.add)
                else:
                    last = v.tensor_tensor(v_rows[:, job - 4, 0:512], job_bank[job][:, :], v_rows[:, job - 4, 0:512],
                                           ALU.add)
                last.then_inc(proj_dve, 1)

            v.wait_ge(same_in, 16 * 6)
            ada_chunk(4)
            ada_chunk(5)
            take_gate(4)
            take_v(4)
            ada_chunk(6)
            take_v(5)
            take_gate(5)

            def take_shift(half):
                v.wait_ge(half_used, 2 * (chunk_no(ADA[6 + half]) + 1))
                at = 4 * half
                v.tensor_tensor(add_f[:, at:at + 4], bank[4][:, 16 + at:20 + at],
                                ba_sb[:, SHIFT_F * KT + at:SHIFT_F * KT + at + 4], ALU.add).then_inc(shift_taken, 1)

            take_shift(0)

            def logits(h):
                v.wait_ge(scores, h + 1)
                if h >= PB:
                    v.wait_ge(p_turned, h - PB + 1)
                hh = head_of(h)
                for t, lo, hi, b0 in ((1, 0, 256, 0), (0, 256, 384, P)):
                    start = BIG if h < NHM else nsink_sb[:, hh - NHM:hh - NHM + 1]
                    last = v.tensor_tensor_reduce(prob[:, h % PB, lo:hi], bank[h % 2][:, lo:hi],
                                                  bias[:, hh, b0:b0 + hi - lo], 1.0, start, ALU.add, ALU.min,
                                                  lowest[:, h, t:t + 1])
                last.then_inc(lows, 1)

            def normalise(h):
                v.wait_ge(exps, h + 1)
                if h >= NHM:
                    link(v.tensor_tensor(rowsum[:, h, :], rowsum[:, h, :], sinkexp[:, h - NHM, :], ALU.add))
                link(v.reciprocal(rowsum[:, h, :], rowsum[:, h, :]))
                v.tensor_scalar(prob[:, h % PB, 0:256], prob[:, h % PB, 0:256], rowsum[:, h, 1:2], None, ALU.mult)
                v.tensor_scalar(prob[:, h % PB, 256:384], prob[:, h % PB, 256:384], rowsum[:, h, 0:1], None, ALU.mult
                                ).then_inc(probs_ready, 1)

            def take_o(blk):
                v.wait_ge(o_ready, 2 * blk + 2)
                to, frm = (ap.rearrange("p (t n) -> p t n", t=TT) for ap in (hT[:, blk, :], bank[6 + blk % 2][:, 0:S]))
                v.tensor_copy(to, frm[:, :, ::-1]).then_inc(o_taken, 1)

            v.wait_ge(bias_in, 16)
            v.wait_ge(wr_in, 16 * 3)
            link(v.tensor_scalar(nsink_sb[:, :], sink_sb[:, :], -1.0, None, ALU.mult))
            for h in range(NH + 4):
                if h < NH:
                    logits(h)
                if 1 <= h <= NH:
                    normalise(h - 1)
                if h >= 5 and h % 2 == 1:
                    take_o((h - 5) // 2)
                if h == 6:
                    take_v(9)
                if h == 9:
                    take_shift(1)

            v.wait_ge(b_out_added, TT)

            def residual(half, t):
                if t == 0:
                    v.wait_ge(mixed, half + 1)
                else:
                    v.wait_ge(half_used, 2 * (chunk_no(("out", half * CW)) + 1))
                cols = slice(half * CW, (half + 1) * CW)
                link(v.tensor_tensor(xn_rows[:, t, cols], mixer_bank[half][t][:, :], gates[:, 0, cols], ALU.mult))
                v.tensor_tensor(x_rows[:, t, cols], x_rows[:, t, cols], xn_rows[:, t, cols], ALU.add
                                ).then_inc(x1_ready, 1)

            def normalise_rows(t):
                v.wait_ge(roots, 2 + t)
                link(v.reciprocal(stat[:, 12 + t:13 + t], stat[:, 10 + t:11 + t]))
                v.tensor_scalar(xn_rows[:, t, :], x_rows[:, t, :], stat[:, 12 + t:13 + t], None, ALU.mult
                                ).then_inc(xn1_ready, 1)

            residual(0, 0)
            residual(0, 1)
            ada_chunk(10)
            residual(1, 0)
            normalise_rows(0)
            residual(1, 1)
            v.wait_ge(half_used, 2 * (chunk_no(ADA[9]) + 1))
            link(v.tensor_tensor(mul_f, bank[2][:, 24:32], ba_sb[:, SCALE_F * KT:(SCALE_F + 1) * KT], ALU.add))
            v.scalar_tensor_tensor(mul_f, mul_f, 1.0, gf_sb, ALU.add, ALU.mult).then_inc(mod_f_ready, 1)
            normalise_rows(1)
            v.wait_ge(mod_f_ready, 1)
            for t in range(TT):
                v.wait_ge(x1_turned, 2 * t + 1)
                for k in range(4):
                    last = v.tensor_scalar(hT[:, k, t * P:(t + 1) * P], turned[t][0][:, k * P:(k + 1) * P],
                                           mul_f[:, k:k + 1], add_f[:, k:k + 1], ALU.mult, ALU.add)
                last.then_inc(h2_dve, 1)
            take_gate(10)

            v.wait_ge(pads, 3)
            for t in range(TT):
                v.wait_ge(logits_ready, t + 1)
                link(v.tensor_tensor(logit[:, t, 0:NE], bank[t][:, 0:NE], br_sb[:, :], ALU.add))
                link(v.max(top8[:, t, :], logit[:, t, 0:NE]))
                v.tensor_scalar(top_stat[:, t, 0:1], top8[:, t, 0:1], -1.0, None, ALU.mult).then_inc(top_ready, 1)
                link(v.memset(top8[:, t, TOPK:8], BIG))
                link(v.match_replace(left[:, t, :], top8[:, t, :], logit[:, t, 0:NE + 4], -BIG))
                v.tensor_tensor(chosen[:, t, :], left[:, t, 0:NE], logit[:, t, 0:NE], ALU.is_lt
                                ).then_inc(chosen_ready, 1)
            v.wait_ge(places, 1)
            first = slot_of[:, :, 0:NE]
            link(v.scalar_tensor_tensor(first, bank[2][:, 0:TT * NE].rearrange("p (t e) -> p t e", t=TT), 2.0 * S,
                                        chosen[:, :, :], ALU.add, ALU.mult))

            def pick_tokens(first):
                for t in range(TT):
                    for i in range(2):
                        last = v.tensor_scalar(pick[:, t, i * SLOTS:(i + 1) * SLOTS], slot_no[:, :],
                                               slot_of[:, t, bass.ds(first + i, 1)], None, ALU.is_equal)
                last.then_inc(picks, 1)

            def weigh_tokens(first):
                for t in range(TT):
                    for i, at in ((0, first), (1, first + 1), (2, first)):
                        v.tensor_scalar(put[:, t, i * SLOTS:(i + 1) * SLOTS], slot_no[:, :],
                                        slot_of[:, t, bass.ds(at, 1)], weight_of[:, t, bass.ds(at, 1)],
                                        ALU.is_equal, ALU.mult)

            def take_xT(b, pairs):
                for k in range(KT):
                    if k % 4 == 0:
                        v.wait_ge(gathered, 2 * pairs + (k // 4 + 1))
                    last = v.tensor_scalar(xT_e[:, b, k, :], (T, Y)[k // 4][:, (k % 4) * P:(k % 4 + 1) * P],
                                           mul_f[:, k:k + 1], add_f[:, k:k + 1], ALU.mult, ALU.add)
                    if k % 4 == 3:
                        last.then_inc(xT_ready, 1)

            def mark_expert(b, e):
                v.tensor_copy(is_expert[:, b, :], ident[:, bass.ds(e, 1)].broadcast_to([P, SLOTS])
                              ).then_inc(is_ready, 1)

            def experts(it, p):
                for e in range(EPB):
                    u, odd = divmod(e, 2)
                    before = it * (3 * EPB) + 3 * e
                    mark_expert((e + 1) % 2, p * EPB + (e + 1))
                    if odd:
                        take_xT((u + 1) % 2, it * 2 + (u + 1))
                    wait_experts(v, it, e, 2)
                    v.tensor_scalar(gate, G[:, :], LIMIT, None, ALU.min).then_inc(gate_cut, 1)
                    v.wait_ge(gate_cut, it * EPB + (e + 1))
                    v.wait_ge(sig_ready, it * EPB + (e + 1))
                    v.tensor_tensor(gate, gate, sig, ALU.mult).then_inc(dve_e, 1)
                    for c, part in enumerate((U, Y)):
                        cols = slice(c * QW, (c + 1) * QW)
                        wait_experts(v, it, e, 3 + c)
                        v.tensor_scalar(up[:, cols], part[:, cols], LIMIT, -LIMIT, ALU.min, ALU.max).then_inc(dve_e, 1)
                        v.wait_ge(dve_e, before + 2 + c)
                        last = v.scalar_tensor_tensor(act[:, cols], up[:, cols], 1.0, gate[:, cols], ALU.add, ALU.mult)
                    last.then_inc(act_ready, 1)
                    if not odd:
                        v.wait_ge(g_turned, it * 2 + (u + 1))
                        pick_tokens(it * EPB + (e + 2))
                        weigh_tokens(it * EPB + (e + 2))
                    wait_experts(v, it, e, 6)
                    if not odd:
                        v.wait_ge(scattered, it * 2 + (u + 1))
                    v.tensor_copy(y_rows[0:SLOTS, odd, :], Y[0:SLOTS, :]).then_inc(y_low_ready, 1)

            pick_tokens(0)
            for t in range(TT):
                v.wait_ge(top_exp, t + 1)
                link(v.tensor_tensor(combine[:, t, :], combine[:, t, :], chosen[:, t, :], ALU.mult))
                link(v.tensor_reduce(top_stat[:, t, 1:2], combine[:, t, :], AX.X, ALU.add))
                link(v.reciprocal(top_stat[:, t, 2:3], top_stat[:, t, 1:2]))
                v.tensor_scalar(combine[:, t, :], combine[:, t, :], top_stat[:, t, 2:3], None, ALU.mult
                                ).then_inc(comb_ready, 1)
            mark_expert(0, 0)
            v.wait_ge(comb_ready, TT)
            for r in range(ROUNDS):
                weights = v.tensor_copy(weight_of[:, :, r * NE:(r + 1) * NE], combine[:, :, :])
            link(weights)
            weigh_tokens(0)
            v.wait_ge(counts, 1)
            v.tensor_reduce(peak[0:1, 0:1], bank[3][0:1, 0:NE], AX.X, ALU.max)
            for r in range(1, ROUNDS):
                last = v.tensor_scalar(slot_of[:, :, r * NE:(r + 1) * NE], first, float(r * SLOTS), None, ALU.subtract)
            last.then_inc(routed, 1)
            take_gate(11)
            take_xT(0, 0)
            v.wait_ge(routed, 1)
            all_rounds(v, experts)

            v.wait_ge(gfin_in, 16)
            for n, (half, t) in enumerate(X2_ORDER):
                v.wait_ge(moe_done, n + 1)
                x2, xg, gt = (a.rearrange("p (c h n) -> p h c n", c=2, h=2)[:, half]
                              for a in (x_rows[:, t, :], xn_rows[:, t, :], gates[:, 1, :]))
                gated = v.tensor_tensor(xg, bank[2 * t + half][:, :].rearrange("p (c n) -> p c n", c=2), gt, ALU.mult)
                if half == 0:
                    gated.then_inc(moe_gated, 1)
                else:
                    link(gated)
                    v.tensor_tensor(x2, x2, xg, ALU.add).then_inc(x2_ready, 1)
            for t in range(TT):
                v.wait_ge(roots, 2 + TT + t)
                link(v.reciprocal(stat[:, 12 + t:13 + t], stat[:, 10 + t:11 + t]))
                v.scalar_tensor_tensor(xn_rows[:, t, :], x_rows[:, t, :], stat[:, 12 + t:13 + t], gfin,
                                       ALU.mult, ALU.mult).then_inc(fin_ready, 1)

        @block.tensor
        def _(pe):
            pe.wait_ge(hot_in, 48)
            pe.matmul(bank[7][0:NH, 0:384], table_sb[:, :], hot_sb, start=True, stop=True).then_inc(line_ready, 1)
            pe.wait_ge(consts, 5)
            for t in range(TT):
                pe.wait_ge(xn_ready, t + 1)
                for half in range(2):
                    for j in range(4):
                        k = 4 * half + j
                        last = pe.transpose(bank[2 * t + half][:, j * P:(j + 1) * P], xn_rows[:, t, k * P:(k + 1) * P],
                                            ident[:, :])
                    last.then_inc(x_turned, 1)

            n = 0
            job = 0

            def columns(n, blocks, job):
                for b0 in range(0, len(blocks), 2):
                    if job == 7:
                        pe.wait_ge(proj_act, 4)
                    for j, w_of in enumerate(blocks[b0:b0 + 2]):
                        for k in range(KT):
                            if job == 0 and j == 0:
                                pe.wait_ge(hT_dve, k + 1)
                                pe.wait_ge(hT_act, k + 1)
                            last = pe.matmul(job_bank[job][:, j * S:(j + 1) * S], w_of(k), hT[:, k, :],
                                             start=(k == 0), stop=(k == KT - 1))
                    last.then_inc(*job_signal(job))
                    job += 1
                return job

            def ada_total(i):
                if i in POOL_ADA:
                    acc = ring[:, chunk_no(ADA[i]) % RING, 0]
                    pe.wait_ge(pool_rows, POOL_ADA.index(i) + 1)
                else:
                    acc = ada_acc[i % 2]
                if i < 4:
                    n = chunk_no(ADA[i])
                    wait_half(pe, n, 1)
                    pe.wait_ge(sc_ready, 1)
                    for m in range(HB):
                        pe.matmul(bank[4][:, 4 * i + m:4 * i + m + 1], ring[:, n % RING, KT - 1, m * P:(m + 1) * P],
                                  sc_sb[:, KT - 1:KT], start=(m == 0), stop=False)
                if i not in POOL_ADA:
                    pe.wait_ge(ada_rows, i + 1 if i < 7 else 8)
                if i in GATE_CHUNKS:
                    if i == 4:
                        pe.wait_ge(proj_act, 1)
                    if i == 5:
                        pe.wait_ge(ada_taken, 1)
                    pe.matmul(gate_bank[i][:, :], ones[:, :], acc, start=True, stop=True).then_inc(half_used, 2)
                else:
                    at = 4 * (i if i < 4 else i - 2)
                    sums = bank[4] if i < 8 else bank[2]
                    for m in range(HB):
                        last = pe.matmul(sums[:, at + m:at + m + 1], acc[:, m * P:(m + 1) * P],
                                         ones[:, 0:1], start=(i >= 4), stop=(i >= 4 or m == HB - 1))
                    last.then_inc(half_used, 2)

            for i in range(4):
                ada_total(i)
            n = 4
            for kind in HEAD_CHUNKS[n:chunk_no(KV_S)]:
                slot = ring[:, n % RING]
                if kind in ADA:
                    ada_total(ADA.index(kind))
                    n += 1
                    continue
                wait_chunk(pe, n)
                if kind in (Q_M, K_M, Q_S):
                    job = columns(n, [lambda k, m=m: slot[:, k, m * P:(m + 1) * P] for m in range(HB)], job)
                else:
                    for t in range(TT):
                        for k in range(KT):
                            last = pe.matmul(job_bank[job][:, :], hT[:, k, t * P:(t + 1) * P], slot[:, k, :],
                                             start=(k == 0), stop=(k == KT - 1))
                        last.then_inc(*job_signal(job))
                        job += 1
                n += 1

            def score(h):
                if h >= 2:
                    pe.wait_ge(lows, h - 1)
                rows = slice(DH * (h % 2), DH * (h % 2) + DH)
                kb = h // 2 if h < NHM else 4
                pe.matmul(bank[h % 2][:, 0:256], qT[rows, h // 2, P:2 * P], kT[rows, kb, :], start=True, stop=True)
                pe.matmul(bank[h % 2][:, 256:384], qT[rows, h // 2, 0:P], kT[rows, kb, 0:P], start=True, stop=True
                          ).then_inc(scores, 1)

            def turn_p(h):
                pe.wait_ge(probs_ready, h + 1)
                if h >= 2:
                    pe.wait_ge(pT_ready, h - 1)
                for to, frm in ((0, 256), (128, 0), (256, 128)):
                    last = pe.transpose(bank[2 + h % 2][:, to:to + P], prob[:, h % PB, frm:frm + P], ident[:, :])
                last.then_inc(p_turned, 1)

            def values(blk):
                pe.wait_ge(pT_ready, 2 * blk + 2)
                if blk >= 2:
                    pe.wait_ge(o_taken, blk - 1)
                if blk == NHM // 2:
                    pe.wait_ge(proj_dve, 3)
                o = bank[6 + blk % 2][:, 0:S]
                for t in range(TT):
                    for half in range(2):
                        h = 2 * blk + half
                        v0 = h * DH if h < NHM else 512 + half * DH
                        last = pe.matmul(o[DH * half:DH * half + DH, t * P:S], v_rows[:, t, v0:v0 + DH],
                                         probT[:, half, 256 * t:256 + 128 * t], start=(t == 0), stop=(t == 1))
                        if t == 1:
                            last.then_inc(o_ready, 1)

            def kv_piece(i):
                n = chunk_no(KV_S)
                w = ring[:, n % RING]
                if i == 0:
                    wait_chunk(pe, n)
                    pe.wait_ge(ada_taken, 2)
                if i == 2:
                    pe.wait_ge(shift_taken, 1)
                if i < 2:
                    for k in range(4 * i, 4 * i + 4):
                        last = pe.matmul(job_bank[8][:, 0:S], w[:, k, 0:P], hT[:, k, :],
                                         start=(k == 0), stop=(k == KT - 1))
                    if i == 1:
                        last.then_inc(*job_signal(8))
                else:
                    t = i - 2
                    for k in range(KT):
                        last = pe.matmul(job_bank[9][:, t * P:(t + 1) * P], hT[:, k, t * P:(t + 1) * P],
                                         w[:, k, P:2 * P], start=(k == 0), stop=(k == KT - 1))
                    if t == 1:
                        last.then_inc(*job_signal(9))

            def project(half, k, t):
                n = chunk_no(("out", half * CW))
                last = pe.matmul(mixer_bank[half][t][:, :], hT[:, k, t * P:(t + 1) * P], ring[:, n % RING, k, :],
                                 start=(k == 0), stop=(k == KT - 1))
                if t == 0 and k == KT - 1:
                    last.then_inc(mixed, 1)
                elif t == 1 and k % HT == HT - 1:
                    last.then_inc(half_used, 1)

            pe.wait_ge(proj_act, 4)
            pe.wait_ge(proj_dve, 2)
            for h in range(NH + 3):
                if h == NHM:
                    pe.wait_ge(proj_act, 7)
                if h < NH:
                    score(h)
                if h == 2:
                    pe.wait_ge(proj_act, 6)
                if 2 <= h < NH + 2:
                    turn_p(h - 2)
                if h in KV_STEPS:
                    kv_piece(KV_STEPS[h])
                if h >= 4 and h % 2 == 0:
                    values((h - 4) // 2)
                for k, t in OUT_STEPS.get(h, ()):
                    if (k, t) == (0, 0):
                        wait_chunk(pe, chunk_no(("out", 0)))
                    if (k, t) == (0, 1):
                        pe.wait_ge(shift_taken, 2)
                    pe.wait_ge(o_taken, k + 1)
                    project(0, k, t)
                if h == 9:
                    pe.wait_ge(proj_dve, 3)
                    ada_total(7)

            for k in range(6, KT):
                pe.wait_ge(o_taken, k + 1)
                for t in range(TT):
                    project(0, k, t)
            ada_total(8)
            wait_chunk(pe, chunk_no(("out", CW)))
            for rows in (range(0, HT), range(HT, KT)):
                for t in range(TT):
                    for k in rows:
                        project(1, k, t)
            ada_total(9)
            for t in range(TT):
                if t == 1:
                    ada_total(10)
                pe.wait_ge(xn1_ready, t + 1)
                for half in range(2):
                    for j in range(4):
                        k = 4 * half + j
                        last = pe.transpose(turned[t][half][:, j * P:(j + 1) * P],
                                            xn_rows[:, t, k * P:(k + 1) * P], ident[:, :])
                    last.then_inc(x1_turned, 1)
            for t in range(TT):
                pe.wait_ge(h2_dve, t + 1)
                for k in range(KT):
                    if k == 4:
                        pe.wait_ge(h2_act, t + 1)
                    last = pe.matmul(bank[t][:, 0:NE], hT[:, k, t * P:(t + 1) * P], wr_sb[:, k, :],
                                     start=(k == 0), stop=(k == KT - 1))
                last.then_inc(logits_ready, 1)
            ada_total(11)
            pe.wait_ge(chosen_ready, 1)
            pe.matmul(bank[2][:, 0:NE], earlier[:, :], chosen[:, 0, :], start=True, stop=True)
            pe.matmul(bank[2][:, NE:2 * NE], ones[:, :], chosen[:, 0, :], start=True, stop=False)
            pe.wait_ge(chosen_ready, TT)
            pe.matmul(bank[2][:, NE:2 * NE], earlier[:, :], chosen[:, 1, :], start=False, stop=True).then_inc(places, 1)
            pe.matmul(bank[3][:, 0:NE], ones[:, :], chosen[:, 0, :], start=True, stop=False)
            pe.matmul(bank[3][:, 0:NE], ones[:, :], chosen[:, 1, :], start=False, stop=True).then_inc(counts, 1)

            total = [[bank[2 * t + half] for half in range(2)] for t in range(TT)]

            def gather(evacuated=None):
                for k in range(KT):
                    if k == 4 and evacuated is not None:
                        pe.wait_ge(y_ready, evacuated)
                        pe.wait_ge(y_low_ready, evacuated)
                    for t in range(TT):
                        last = pe.matmul((T, Y)[k // 4][:, (k % 4) * P:(k % 4 + 1) * P], xn_rows[:, t, k * P:(k + 1) * P],
                                         pick[:, t, :], start=(t == 0), stop=(t == TT - 1))
                    if k % 4 == 3:
                        last.then_inc(gathered, 1)

            def scatter(stop):
                for t in range(TT):
                    for half in range(2):
                        last = pe.matmul(total[t][half][:, :], gT[:, t, half, :], y_rows[:, half, :],
                                         start=False, stop=stop)
                        if stop:
                            last.then_inc(moe_done, 1)
                if not stop:
                    last.then_inc(scattered, 1)

            def products(e, it, g, banks, second_half):
                odd = e % 2
                for c in range(2):
                    n = PRE + CPE * e + 2 * g + c
                    to = banks[c]
                    for k in range(KT):
                        if k % HT == 0:
                            wait_half(pe, n, k // HT, it)
                        if c == 0 and k == HT and second_half is not None:
                            pe.wait_ge(xT_ready, second_half)
                        if k == HT:
                            for half in range(2):
                                col0 = g * FF + c * CW + half * QW
                                pe.matmul(to[half * SLOTS:(half + 1) * SLOTS, c * QW:(c + 1) * QW],
                                          is_expert[:, e % 2, :], bgu[:, col0:col0 + QW], start=False, stop=False)
                        for half in range(2):
                            last = pe.matmul(to[half * SLOTS:(half + 1) * SLOTS, c * QW:(c + 1) * QW],
                                             xT_e[:, e // 2 % 2, k, odd * SLOTS:(odd + 1) * SLOTS],
                                             ring[:, n % RING, k, half * QW:(half + 1) * QW],
                                             start=(k == 0), stop=(k == KT - 1))
                        if k % HT == HT - 1:
                            last.then_inc(half_used, 1)

            def begin_totals():
                pe.wait_ge(combT_ready, 1)
                pe.wait_ge(bdown_in, 16)
                pe.wait_ge(routed, 1)
                for t in range(TT):
                    for c in range(2):
                        for half in range(2):
                            pe.matmul(total[t][half][:, c * QW:(c + 1) * QW], combT[:, t * P:(t + 1) * P],
                                      bdown_sb[:, c * CW + half * QW:c * CW + (half + 1) * QW],
                                      start=(c == 0), stop=False)

            def experts(it, p, opening=False):
                for e in range(EPB):
                    u, odd = divmod(e, 2)
                    first = PRE + CPE * e
                    pe.wait_ge(is_ready, it * EPB + (e + 1))
                    half_of_xT = 2 * (it * 2 + u)
                    if not odd:
                        pe.wait_ge(xT_ready, half_of_xT + 1)
                    if odd:
                        pe.wait_ge(picks, it * 2 + (u + 2))
                        gather(it * EPB + e)
                    products(e, it, 0, (G, G), None if odd else half_of_xT + 2)
                    if not odd:
                        if opening and u == 1:
                            begin_totals()
                        if not (opening and u == 0):
                            pe.wait_ge(y_ready, it * EPB + e)
                            pe.wait_ge(y_low_ready, it * EPB + e)
                            pe.wait_ge(gT_ready, it * 2 + u)
                            scatter(False)
                        pe.wait_ge(gate_cut, it * EPB + (e + 1))
                        for t in range(TT):
                            for s in range(2):
                                last = pe.transpose(G[:, (2 * t + s) * P:(2 * t + s + 1) * P],
                                                    put[:, t, s * SLOTS:s * SLOTS + P], ident[:, :])
                        last.then_inc(g_turned, 1)
                    if opening and e == 0:
                        pe.wait_ge(combT_ready, 1)
                    if odd:
                        pe.wait_ge(xT_ready, half_of_xT + 4)
                    products(e, it, 1, (U, Y), None)
                    pe.wait_ge(act_ready, it * EPB + (e + 1))
                    for j in range(4):
                        last = pe.transpose(T[:, j * P:(j + 1) * P], act[:, j * P:(j + 1) * P], ident[:, :])
                    last.then_inc(act_turned, 1)
                    pe.wait_ge(actT_ready, it * EPB + (e + 1))
                    for c in range(2):
                        n = first + 4 + c
                        for k in range(KT):
                            if k % HT == 0:
                                wait_half(pe, n, k // HT, it)
                            blk, part = 2 * (k // 4) + k % 2, k % 4 // 2
                            for half in range(2):
                                rows = half ^ odd
                                last = pe.matmul(Y[rows * SLOTS:(rows + 1) * SLOTS, c * QW:(c + 1) * QW],
                                                 actT[:, blk * P + part * SLOTS:blk * P + (part + 1) * SLOTS],
                                                 ring[:, n % RING, k, half * QW:(half + 1) * QW],
                                                 start=(k == 0), stop=(k == KT - 1))
                            if k % HT == HT - 1:
                                last.then_inc(half_used, 1)

            pe.wait_ge(picks, 1)
            gather()
            pe.wait_ge(comb_ready, TT)
            for t in range(TT):
                pe.transpose(U[0:NE, t * P:(t + 1) * P], combine[:, t, :], ident[:, :]
                             ).then_inc(comb_turned if t else scattered, 1)
            pe.wait_ge(bgu_in, 16)
            experts(0, 0, opening=True)
            bodies = all_rounds(pe, experts, begin=1)
            pe.wait_ge(y_ready, bodies * EPB)
            pe.wait_ge(y_low_ready, bodies * EPB)
            pe.wait_ge(gT_ready, bodies * 2)
            scatter(True)


def kernel(x, c, g_attn, w_ada, b_ada, w_in, b_in, w_out, b_out, rel_table, sinks, g_ffn, w_router, b_router,
           w_gate_up, b_gate_up, w_down, b_down, g_final):
    import concourse.bacc as bacc
    from concourse.bass_utils import run_bass_kernel_spmd

    def columns(a, tiles):
        return np.ascontiguousarray(np.asarray(a).reshape(tiles, P).T)

    b_in_0 = np.asarray(b_in)[0]
    swa_q = b_in_0[1536:2048].reshape(2, 4, DH).transpose(1, 0, 2).reshape(-1)
    b_in_blocks = np.concatenate([b_in_0[:1536], swa_q, b_in_0[2048:]])
    w_q = np.asarray(w_in)[0]
    w_q = np.concatenate([w_q[:, :1536], w_q[:, 1536:2048].reshape(D, 2, 4, DH).transpose(0, 2, 1, 3).reshape(D, 512),
                          w_q[:, 2048:]], axis=1)
    w_o = np.asarray(w_out)[0]
    w_o = np.concatenate([w_o[:512], w_o[512:].reshape(2, 4, DH, D).transpose(1, 0, 2, 3).reshape(512, D)])

    arrays = {
        "x": np.asarray(x)[0],
        "vectors": np.concatenate([columns(c, KT), columns(g_attn, KT), columns(g_ffn, KT), columns(b_ada, 6 * KT),
                                   columns(b_in_blocks, D_IN // P)], axis=1),
        "w_ada": np.asarray(w_ada)[0], "b_ada_row": np.asarray(b_ada)[0],
        "w_in": w_q, "b_in_row": b_in_0,
        "w_out": w_o, "b_out": np.asarray(b_out)[0], "rel_table": np.asarray(rel_table), "sinks": np.asarray(sinks)[0],
        "w_router": np.asarray(w_router)[0], "b_router": np.asarray(b_router)[0],
        "w_gate_up": np.asarray(w_gate_up)[0],
        "b_gate_up": np.asarray(b_gate_up)[0],
        "w_down": np.asarray(w_down)[0], "b_down": np.asarray(b_down)[0], "g_final": np.asarray(g_final),
        "bucket_hot": bucket_table(), "masks": mask_rows(),
    }
    arrays = {name: np.ascontiguousarray(a) for name, a in arrays.items()}
    nc = bacc.Bacc("TRN2", target_bir_lowering=False, num_devices=1)
    args = {name: nc.dram_tensor(name, a.shape, mybir.dt.from_np(a.dtype), kind="ExternalInput").ap()
            for name, a in arrays.items()}
    toeplitz = nc.dram_tensor("bias_lines", [NH, 384], F32, kind="Internal").ap()
    out = nc.dram_tensor("out", [S, D], F32, kind="ExternalOutput").ap()
    build(nc, **args, toeplitz=toeplitz, out=out)
    result = run_bass_kernel_spmd(nc, [arrays], core_ids=[0])
    return result.results[0]["out"].reshape(1, S, D)
```
